# Optimizing a Trainium2 kernel written in Bass

```python
import jax, jax.numpy as jnp
from jax import lax
import numpy as np

D_MODEL = 1024
BATCH = 1
SEQ = 128
DEPTH = 2
DEC_BATCH = 1
DEC_SEQ = 256
PAST_LEN = 128

GRID_W = 64
N_Q_HEADS = 8
N_KV_HEADS = 2
GQA_GROUP = N_Q_HEADS // N_KV_HEADS
HEAD_DIM = 64
AXIS_DIM = HEAD_DIM // 2
ATTN_WIDTH = N_Q_HEADS * HEAD_DIM
KV_WIDTH = N_KV_HEADS * HEAD_DIM
ROPE_THETA = 10000.0
Q_BLOCK = 128
HGRN_HEADS = 4
HGRN_K = 128
HGRN_V = 128
HGRN_WIDTH = HGRN_HEADS * HGRN_K
HGRN_CHUNK = 64
N_EXPERTS = 16
N_GROUPS = 4
EXPERTS_PER_GROUP = N_EXPERTS // N_GROUPS
TOP_K = 2
D_FF = 512
EPS = 1e-6
IN_WIDTHS = (ATTN_WIDTH, KV_WIDTH, KV_WIDTH, HGRN_WIDTH, HGRN_WIDTH, HGRN_WIDTH, HGRN_WIDTH, HGRN_WIDTH, D_MODEL, D_MODEL)
IN_COLS = ATTN_WIDTH + 2 * KV_WIDTH + 5 * HGRN_WIDTH + 2 * D_MODEL

kernel_name = 'hybrid_gqa_hgrn2_moe_diffusion_step'

F32 = jnp.float32

def split_points():
    pts, acc = [], 0
    for w in IN_WIDTHS[:-1]:
        acc += w
        pts.append(acc)
    return pts

def rms_norm(x, w):
    xf = x.astype(F32)
    y = xf * lax.rsqrt(jnp.mean(xf * xf, axis=-1, keepdims=True) + EPS)
    return (y * w.astype(F32)).astype(x.dtype)

def modulation(silu_cond, w_mod_l, b_mod_l):
    m = silu_cond @ w_mod_l + b_mod_l
    return jnp.split(m[:, None, :], 6, axis=-1)

def modulate(x, w, shift, scale):
    return rms_norm(x, w) * (1 + scale) + shift

def axial_rope_tables(n_tokens):
    rows = n_tokens // GRID_W
    row_ids = jnp.repeat(jnp.arange(rows), GRID_W).astype(F32)
    col_ids = jnp.tile(jnp.arange(GRID_W), rows).astype(F32)
    inv_freq = ROPE_THETA ** (-jnp.arange(0, AXIS_DIM, 2, dtype=F32) / AXIS_DIM)
    ang_r = row_ids[:, None] * inv_freq[None, :]
    ang_c = col_ids[:, None] * inv_freq[None, :]
    ang = jnp.concatenate([ang_r, ang_r, ang_c, ang_c], axis=-1)
    return jnp.cos(ang), jnp.sin(ang)

def apply_axial_rope(x, cos, sin):
    quarter = AXIS_DIM // 2

    def rot_half(u):
        return jnp.concatenate([-u[..., quarter:], u[..., :quarter]], axis=-1)

    rotated = jnp.concatenate([rot_half(x[..., :AXIS_DIM]), rot_half(x[..., AXIS_DIM:])], axis=-1)
    return (x.astype(F32) * cos + rotated.astype(F32) * sin).astype(x.dtype)

def block_attention(q, k, v):
    b, hkv, g, t, hd = q.shape
    nb = t // Q_BLOCK
    qb = q.reshape(b, hkv, g, nb, Q_BLOCK, hd).transpose(3, 0, 1, 2, 4, 5)
    kf, vf = k.astype(F32), v.astype(F32)
    scale = hd ** -0.5

    def one_block(qblk):
        s = jnp.einsum('bhgqd,bhkd->bhgqk', qblk.astype(F32), kf) * scale
        p = jax.nn.softmax(s, axis=-1)
        return jnp.einsum('bhgqk,bhkd->bhgqd', p, vf).astype(q.dtype)

    out = lax.map(one_block, qb)
    return out.transpose(1, 2, 3, 0, 4, 5).reshape(b, hkv * g, t, hd)

def hgrn_chunk_scan(q, k, v, log_f, s0):
    b, h, t, _ = q.shape
    dv = v.shape[-1]
    nc = t // HGRN_CHUNK

    def to_chunks(a):
        return a.reshape(b, h, nc, HGRN_CHUNK, a.shape[-1]).transpose(2, 0, 1, 3, 4).astype(F32)

    incl = jnp.tril(jnp.ones((HGRN_CHUNK, HGRN_CHUNK), dtype=bool))[:, :, None]

    def step(state, blk):
        qc, kc, vc, gc = blk
        bcum = jnp.cumsum(gc, axis=2)
        o_inter = jnp.einsum('bhck,bhkv->bhcv', qc * jnp.exp(bcum), state)
        diff = bcum[:, :, :, None, :] - bcum[:, :, None, :, :]
        decay = jnp.exp(jnp.where(incl, diff, -jnp.inf))
        scores = jnp.einsum('bhtk,bhsk,bhtsk->bhts', qc, kc, decay)
        o_intra = jnp.einsum('bhts,bhsv->bhtv', scores, vc)
        b_last = bcum[:, :, -1:, :]
        k_dec = kc * jnp.exp(b_last - bcum)
        new_state = jnp.exp(b_last[:, :, 0, :])[..., None] * state + jnp.einsum('bhsk,bhsv->bhkv', k_dec, vc)
        return new_state, o_inter + o_intra

    s_final, o = lax.scan(step, s0.astype(F32), (to_chunks(q), to_chunks(k), to_chunks(v), to_chunks(log_f)))
    return o.transpose(1, 2, 0, 3, 4).reshape(b, h, t, dv), s_final

def layer_lower_bounds(lb_logits):
    p = jax.nn.softmax(lb_logits.astype(F32), axis=0)
    return jnp.cumsum(p, axis=0) - p[0:1]

def hgrn_branch(h_q, h_ff, h_fb, h_i, h_g, lb_f, lb_b, hnorm_w, s0_f, s0_b):
    b, t, _ = h_q.shape

    def heads(a, d):
        return a.reshape(b, t, HGRN_HEADS, d).transpose(0, 2, 1, 3)

    q = heads(jax.nn.silu(h_q.astype(F32)), HGRN_K) * (HGRN_K ** -0.5)
    v = heads(h_i.astype(F32), HGRN_V)

    def gates(hf, lb):
        f = lb + (1.0 - lb) * jax.nn.sigmoid(hf.astype(F32))
        return heads(1.0 - f, HGRN_K), heads(jnp.log(f), HGRN_K)

    k_f, lf_f = gates(h_ff, lb_f)
    k_b, lf_b = gates(h_fb, lb_b)
    o_f, s_f = hgrn_chunk_scan(q, k_f, v, lf_f, s0_f)

    def flip(a):
        return jnp.flip(a, axis=2)

    o_b, s_b = hgrn_chunk_scan(flip(q), flip(k_b), flip(v), flip(lf_b), s0_b)
    o = o_f + flip(o_b)
    o = rms_norm(o, hnorm_w) * jax.nn.silu(heads(h_g.astype(F32), HGRN_V))
    o = o.transpose(0, 2, 1, 3).reshape(b, t, HGRN_WIDTH).astype(h_q.dtype)
    return o, s_f, s_b

def token_mixer(h, lw, rope, ctx):
    b, t, _ = h.shape
    a_q, a_k, a_v, h_q, h_ff, h_fb, h_i, h_g, g_attn, g_hgrn = jnp.split(h @ lw['w_in'], split_points(), axis=-1)
    q = rms_norm(a_q.reshape(b, t, N_Q_HEADS, HEAD_DIM), lw['q_norm']).transpose(0, 2, 1, 3)
    k = rms_norm(a_k.reshape(b, t, N_KV_HEADS, HEAD_DIM), lw['k_norm']).transpose(0, 2, 1, 3)
    v = a_v.reshape(b, t, N_KV_HEADS, HEAD_DIM).transpose(0, 2, 1, 3)
    if ctx is None:
        keys, vals = k, v
        s0_f = jnp.zeros((b, HGRN_HEADS, HGRN_K, HGRN_V), F32)
        s0_b = jnp.zeros((b, HGRN_HEADS, HGRN_K, HGRN_V), F32)
    else:
        ctx_k, ctx_v, s0_f, s0_b = ctx
        cos, sin = rope
        q = apply_axial_rope(q, cos, sin)
        k = apply_axial_rope(k, cos, sin)
        keys = jnp.concatenate([k, ctx_k.astype(k.dtype)], axis=2)
        vals = jnp.concatenate([v, ctx_v.astype(v.dtype)], axis=2)
    attn = block_attention(q.reshape(b, N_KV_HEADS, GQA_GROUP, t, HEAD_DIM), keys, vals)
    attn = attn.transpose(0, 2, 1, 3).reshape(b, t, ATTN_WIDTH)
    rec, s_f, s_b = hgrn_branch(h_q, h_ff, h_fb, h_i, h_g, lw['lb_f'], lw['lb_b'], lw['hnorm'], s0_f, s0_b)
    merged = (jax.nn.sigmoid(g_attn) * (attn @ lw['w_br_attn'])
              + jax.nn.sigmoid(g_hgrn) * (rec @ lw['w_br_hgrn']))
    return merged @ lw['w_out'], (k, v, s_f, s_b)

def moe_ffn(h, lw):
    b, t, d = h.shape
    xt = h.reshape(b * t, d)
    scores = jax.nn.sigmoid((xt @ lw['w_router']).astype(F32))
    sel = scores + lw['b_router'].astype(F32)
    grp_score = lax.top_k(sel.reshape(-1, N_GROUPS, EXPERTS_PER_GROUP), TOP_K)[0].sum(-1)
    best = jnp.argmax(grp_score, axis=-1)
    in_group = (jnp.arange(N_EXPERTS) // EXPERTS_PER_GROUP)[None, :] == best[:, None]
    _, idx = lax.top_k(jnp.where(in_group, sel, -jnp.inf), TOP_K)
    w = jnp.take_along_axis(scores, idx, axis=-1)
    w = w / jnp.sum(w, axis=-1, keepdims=True)
    gates = jnp.sum(jax.nn.one_hot(idx, N_EXPERTS, dtype=F32) * w[..., None], axis=1)
    act = jax.nn.silu(jnp.einsum('nd,edf->nef', xt, lw['w_gate'])) * jnp.einsum('nd,edf->nef', xt, lw['w_up'])
    y = jnp.einsum('nef,efd->nd', act * gates[..., None].astype(act.dtype), lw['w_down'])
    return y.reshape(b, t, d)

def run_layer(x, silu_cond, lw, rope, ctx):
    sh1, sc1, g1, sh2, sc2, g2 = modulation(silu_cond, lw['w_mod'], lw['b_mod'])
    out, ctx_tensors = token_mixer(modulate(x, lw['norm1'], sh1, sc1), lw, rope, ctx)
    x = x + g1 * out
    x = x + g2 * moe_ffn(modulate(x, lw['norm2'], sh2, sc2), lw)
    return x, ctx_tensors

def setup_inputs(seed: int = 0) -> dict:
    key = jax.random.key(seed)
    ks = jax.random.split(key, 32)

    def nrm(k, shape, scale=1.0):
        return jax.random.normal(k, shape, F32) * scale

    return {
        'x_prompt': nrm(ks[0], (BATCH, SEQ, D_MODEL)),
        'x_sample': nrm(ks[1], (DEC_BATCH, DEC_SEQ, D_MODEL)),
        'cache_k': nrm(ks[2], (DEC_BATCH, DEPTH, N_KV_HEADS, PAST_LEN, HEAD_DIM)),
        'cache_v': nrm(ks[3], (DEC_BATCH, DEPTH, N_KV_HEADS, PAST_LEN, HEAD_DIM)),
        'state_fwd': nrm(ks[4], (DEC_BATCH, DEPTH, HGRN_HEADS, HGRN_K, HGRN_V), 0.5),
        'state_bwd': nrm(ks[5], (DEC_BATCH, DEPTH, HGRN_HEADS, HGRN_K, HGRN_V), 0.5),
        'c': nrm(ks[6], (DEC_BATCH, D_MODEL)),
        'c_ctx': nrm(ks[7], (D_MODEL,)),
        'norm1_w': 1.0 + nrm(ks[8], (DEPTH, D_MODEL), 0.02),
        'norm2_w': 1.0 + nrm(ks[9], (DEPTH, D_MODEL), 0.02),
        'w_mod': nrm(ks[10], (DEPTH, D_MODEL, 6 * D_MODEL), 0.5 * D_MODEL ** -0.5),
        'b_mod': nrm(ks[11], (DEPTH, 6 * D_MODEL), 0.02),
        'w_in': nrm(ks[12], (DEPTH, D_MODEL, IN_COLS), D_MODEL ** -0.5),
        'q_norm_w': 1.0 + nrm(ks[13], (DEPTH, HEAD_DIM), 0.02),
        'k_norm_w': 1.0 + nrm(ks[14], (DEPTH, HEAD_DIM), 0.02),
        'hgrn_lb_fwd': 1.0 + nrm(ks[15], (DEPTH, HGRN_WIDTH), 0.1),
        'hgrn_lb_bwd': 1.0 + nrm(ks[16], (DEPTH, HGRN_WIDTH), 0.1),
        'hgrn_norm_w': 1.0 + nrm(ks[17], (DEPTH, HGRN_V), 0.02),
        'w_br_attn': nrm(ks[18], (DEPTH, ATTN_WIDTH, D_MODEL), ATTN_WIDTH ** -0.5),
        'w_br_hgrn': nrm(ks[19], (DEPTH, HGRN_WIDTH, D_MODEL), HGRN_WIDTH ** -0.5),
        'w_out': nrm(ks[20], (DEPTH, D_MODEL, D_MODEL), D_MODEL ** -0.5),
        'w_router': nrm(ks[21], (D_MODEL, N_EXPERTS), D_MODEL ** -0.5),
        'b_router': nrm(ks[22], (N_EXPERTS,), 0.01),
        'w_exp_gate': nrm(ks[23], (DEPTH, N_EXPERTS, D_MODEL, D_FF), D_MODEL ** -0.5),
        'w_exp_up': nrm(ks[24], (DEPTH, N_EXPERTS, D_MODEL, D_FF), D_MODEL ** -0.5),
        'w_exp_down': nrm(ks[25], (DEPTH, N_EXPERTS, D_FF, D_MODEL), D_FF ** -0.5),
    }

def reference(x_prompt, x_sample, cache_k, cache_v, state_fwd, state_bwd, c, c_ctx,
              norm1_w, norm2_w, w_mod, b_mod, w_in, q_norm_w, k_norm_w, hgrn_lb_fwd, hgrn_lb_bwd,
              hgrn_norm_w, w_br_attn, w_br_hgrn, w_out, w_router, b_router,
              w_exp_gate, w_exp_up, w_exp_down):
    lb_f_all = layer_lower_bounds(hgrn_lb_fwd)
    lb_b_all = layer_lower_bounds(hgrn_lb_bwd)

    def layer_weights(l):
        return {'norm1': norm1_w[l], 'norm2': norm2_w[l], 'w_mod': w_mod[l], 'b_mod': b_mod[l],
                'w_in': w_in[l], 'q_norm': q_norm_w[l], 'k_norm': k_norm_w[l],
                'lb_f': lb_f_all[l], 'lb_b': lb_b_all[l], 'hnorm': hgrn_norm_w[l],
                'w_br_attn': w_br_attn[l], 'w_br_hgrn': w_br_hgrn[l], 'w_out': w_out[l],
                'w_router': w_router, 'b_router': b_router,
                'w_gate': w_exp_gate[l], 'w_up': w_exp_up[l], 'w_down': w_exp_down[l]}

    silu_ctx = jax.nn.silu(c_ctx)[None, :]
    xp = x_prompt
    ks_out, vs_out, sf_out, sb_out = [], [], [], []
    for l in range(DEPTH):
        xp, (kc, vc, sf, sb) = run_layer(xp, silu_ctx, layer_weights(l), None, None)
        ks_out.append(kc)
        vs_out.append(vc)
        sf_out.append(sf)
        sb_out.append(sb)
    new_cache_k = jnp.stack(ks_out, axis=1)
    new_cache_v = jnp.stack(vs_out, axis=1)
    new_state_fwd = jnp.stack(sf_out, axis=1)
    new_state_bwd = jnp.stack(sb_out, axis=1)

    rope = axial_rope_tables(x_sample.shape[1])
    silu_c = jax.nn.silu(c)
    xs = x_sample
    for l in range(DEPTH):
        ctx = (cache_k[:, l], cache_v[:, l], state_fwd[:, l], state_bwd[:, l])
        xs, _ = run_layer(xs, silu_c, layer_weights(l), rope, ctx)

    return (xp, xs, new_cache_k, new_cache_v, new_state_fwd, new_state_bwd)


_drawn_inputs = setup_inputs


def setup_inputs(seed=0):
    import zlib

    import numpy as np

    out = dict(_drawn_inputs(seed))
    spreads = {}
    factors = {'cache_k': 3.142,
     'state_fwd': 8.0,
     'state_bwd': 8.0,
     'norm1_w': 2.798,
     'q_norm_w': 8.0,
     'k_norm_w': 2.86,
     'hgrn_norm_w': 4.239}
    for name, (base, spread) in spreads.items():
        noise = np.random.default_rng([zlib.crc32(name.encode()), seed]).standard_normal(out[name].shape)
        drawn = base * np.exp(spread * noise) if base else spread * noise
        out[name] = __import__('jax').numpy.asarray(drawn.astype(out[name].dtype))
    for name, factor in factors.items():
        out[name] = (out[name] * factor).astype(out[name].dtype)
    return out
```

```python
from contextlib import ExitStack

import numpy as np

import concourse.bass as bass
from concourse import mybir

F32 = mybir.dt.float32
I32 = mybir.dt.int32
U8 = mybir.dt.uint8
ALU = mybir.AluOpType
ACT = mybir.ActivationFunctionType
AX = mybir.AxisListType

P = 128
D = 1024
KC = D // P
NT = 3
TOK = NT * P
DEPTH = 2
NQ, NKV, HD = 8, 2, 64
HH, HK = 4, 128
SEG = HH * NT
NE, NG, EPG = 16, 4, 4
FF = 512
BLK = 64
EPS = 1e-6
GRID_W = 64
ROPE_THETA = 10000.0
MAX_EXTRA = 12
YROWS = (NE + MAX_EXTRA) * BLK
FAR = 10000.0
NGATH = NE + 1
NPOS = NE + 2

MIX_UNITS = ([("mod", m) for m in range(4)]
             + [("q", 0), ("kv", 0), ("hq", 0), ("ff", 0), ("fb", 0), ("i", 0), ("g", 0), ("ga", 0), ("ga", 1)]
             + [("mod", m) for m in range(4, 12)]
             + [("wba", 0), ("gh", 0), ("gh", 1), ("wbh", 0), ("wo", 0), ("wo", 1)])
MIX_SLOTS = 4
UNIT_NO = {u: n for n, u in enumerate(MIX_UNITS)}
NU = len(MIX_UNITS)
LAST_GROUP = {"q": NT - 1, "kv": NT - 1, "hq": HH - 1, "ff": HH - 1, "fb": HH - 1, "i": NT - 1, "g": NT - 1,
              "wba": KC - 1, "wbh": KC - 1}


def last_group(unit):
    kind, i = unit
    if kind == "mod":
        return unit
    if kind in ("ga", "gh"):
        return kind, 4 * i + 3
    return kind, NT * (i + 1) - 1 if kind == "wo" else LAST_GROUP[kind]


SLOT_LOADS = [len([n for n in range(NU) if n % MIX_SLOTS == s]) if s < MIX_SLOTS else 0 for s in range(6)]
COL0 = {("q", 0): 0, ("kv", 0): 512, ("hq", 0): 768, ("ff", 0): 1280, ("fb", 0): 1792, ("i", 0): 2304,
        ("g", 0): 2816, ("ga", 0): 3328, ("ga", 1): 3840, ("gh", 0): 4352, ("gh", 1): 4864}

GROUPS = ([("mod", m) for m in range(4)]
          + [("q", t) for t in range(NT)] + [("kv", t) for t in range(NT)]
          + [("hq", h) for h in range(HH)] + [("ff", h) for h in range(HH)] + [("fb", h) for h in range(HH)]
          + [("i", t) for t in range(NT)] + [("g", t) for t in range(NT)]
          + [("ga", j) for j in range(KC)] + [("mod", m) for m in range(4, 12)]
          + [("wba", j) for j in range(KC)]
          + [(k, j) for j in range(KC) for k in ("gh", "wbh")]
          + [("wo", n) for n in range(2 * NT)])
GROUP_NO = {g: n for n, g in enumerate(GROUPS)}
NGR = len(GROUPS)
assert NGR % 2 == 0
ATT_STEPS = 4 * NT
ATT_AT = {g: k for k, g in enumerate([("hq", 3)] + [("ff", h) for h in range(HH)] + [("fb", h) for h in range(HH)]
                                     + [("i", t) for t in range(NT)] + [("g", 0), ("g", 1)])}
NLEV = 7
LEV_STEPS = 2 * NLEV + 1
LEV_AT = {g: k for k, g in enumerate([("ga", j) for j in range(KC)] + [("mod", m) for m in range(4, 11)])}
LEV_TILES = LEV_STEPS * NT

O_BANK = (6, 7, 2)
SMALL_LOADS = 16 * 11
Y0 = 16 * (MAX_EXTRA * BLK // P) // 3

C_ID, C_TRI, C_ONE, C_IOTA, C_E64, C_OB, C_BEFORE, C_COS, C_SIN = 0, 128, 256, 384, 448, 464, 480, 496, 624
NCONST = 752


def shape_constants():
    c = np.zeros((P, NCONST), np.float32)
    c[:, C_ID:C_ID + P] = np.eye(P)
    c[:, C_TRI:C_TRI + P] = np.triu(np.ones((P, P)), 1)
    c[:, C_ONE:C_ONE + P] = 1.0
    c[:, C_IOTA:C_IOTA + BLK] = np.arange(BLK)
    c[:, C_E64:C_E64 + NE] = BLK * np.arange(NE)
    c[:, C_OB:C_OB + NE] = (NE - 1) * BLK - BLK * np.arange(NE)
    c[:, C_BEFORE:C_BEFORE + 16] = np.tril(np.ones((4, 4)), -1).reshape(-1)
    tok = np.arange(2 * P)
    inv = np.float32(ROPE_THETA) ** (-np.arange(0, 32, 2, dtype=np.float32) / np.float32(32))
    ar = (tok // GRID_W).astype(np.float32)[:, None] * inv
    ac = (tok % GRID_W).astype(np.float32)[:, None] * inv
    ang = np.concatenate([ar, ar, ac, ac], 1)
    sign = np.tile(np.repeat([-1.0, 1.0], 16), 2).astype(np.float32)
    for t in range(2):
        c[:, C_COS + HD * t:C_COS + HD * (t + 1)] = np.cos(ang[t * P:(t + 1) * P])
        c[:, C_SIN + HD * t:C_SIN + HD * (t + 1)] = np.sin(ang[t * P:(t + 1) * P]) * sign
    masks = np.zeros((P, LEV_STEPS, P), np.int32)
    s, t = np.arange(P)[:, None], np.arange(P)[None, :]
    for lev in range(NLEV):
        m = 64 >> lev
        same = (s // (2 * m)) == (t // (2 * m))
        masks[:, 2 * lev] = same & (s % (2 * m) < m) & (t % (2 * m) >= m)
        masks[:, 2 * lev + 1] = same & (s % (2 * m) >= m) & (t % (2 * m) < m)
    masks[:, 2 * NLEV] = s == t
    return c, masks.reshape(P, -1)


def build(nc, a, o):
    y_prompt, y_sample, new_k, new_v, new_sf, new_sb = o
    mod_scr = nc.dram_tensor("mod_scr", [DEPTH, 2, 6 * D], F32, kind="Internal").ap()
    y_scr = nc.dram_tensor("y_scr", [YROWS, D], F32, kind="Internal").ap()

    with ExitStack() as ctx:
        def sb(name, shape, dt=F32):
            return ctx.enter_context(nc.sbuf_tensor(name, shape, dt))

        def sem(name):
            return ctx.enter_context(nc.semaphore(name))

        ring = sb("ring", [P, 6, 4096])
        xs = sb("xs", [P, NT, D])
        hrow = sb("hrow", [P, NT, D])
        hT = sb("hT", [P, KC, TOK])
        modb = sb("modb", [P, 3, 2, D])
        nw = sb("nw", [P, D])
        gen = sb("gen", [P, 9240])
        const = sb("const", [P, NCONST])
        masks = sb("masks", [P, LEV_STEPS, P], U8)
        prow = sb("prow", [32, P])
        lbT = sb("lbT", [P, DEPTH, 2, HH])
        omT = sb("omT", [P, DEPTH, 2, HH])
        lbe = sb("lbe", [P, 4, 8])
        qnw = sb("qnw", [P, DEPTH, HD])
        knw = sb("knw", [P, DEPTH, HD])
        hnw = sb("hnw", [P, DEPTH, HK])
        cst = sb("cst", [P, KC, 2, 16])
        brow = sb("brow", [P, P])
        wr = sb("wr", [P, KC, NE])
        br = sb("br", [P, NE])
        stat = sb("stat", [P, 96])
        dec = sb("dec", [P, 2, SEG])
        lraw = sb("lraw", [P, 16])
        half = sb("half", [P, 16])
        idx = sb("idx", [P, 2, NT], I32)
        wgt = sb("wgt", [P, 2, NT])
        nov = sb("nov", [1, NE], I32)
        mstage = sb("mstage", [P, 2, P])

        ident = const[:, C_ID:C_ID + P]
        tri = const[:, C_TRI:C_TRI + P]
        ones = const[:, C_ONE:C_ONE + P]
        iota = const[:, C_IOTA:C_IOTA + BLK]

        S = ring[:, 4:6, :].rearrange("p a b -> p (a b)")
        Q = S[:, 0:1536].rearrange("p (t c) -> p t c", t=NT)
        sg = Q
        Kd = S[:, 1536:2560].rearrange("p (b g u d) -> p b g u d", b=4, g=NKV, u=2)
        Vt = S[:, 2560:3072].rearrange("p (b c) -> p b c", b=4)
        qTa = S[:, 3072:4608].rearrange("p (r t) -> p r t", r=4)
        kT = S[:, 4608:5632].rearrange("p (g k) -> p g k", g=NKV)
        prob = S[:, 5632:7168].rearrange("p (b u k) -> p b u k", b=2, u=2)
        PT = S[:, 7168:7936].rearrange("p (u k) -> p u k", u=2)
        AT = S[:, 1536:3072].rearrange("p (s t) -> p s t", s=SEG)
        E = [S[:, 3072:4608], S[:, 4608:6144]]
        orow = E[1].rearrange("p (t c) -> p t c", t=NT)
        MB = modb[:, 0:2].rearrange("p a b c -> p (a b c)")
        attnT = MB[:, 0:1536].rearrange("p (r t) -> p r t", r=4)
        W = [S[:, 6144:7680], MB[:, 1536:3072]]
        St = MB[:, 3072:4096].rearrange("p (d h v) -> p d h v", d=2, h=HH)
        scratch = W[1]
        qh = gen[:, 0:1536]
        kg = [gen[:, 1536:3072], gen[:, 3072:4608]]
        Cflat = [gen[:, 4608:6156], gen[:, 6156:7704]]
        Cs = [c.rearrange("p (s t) -> p s t", s=SEG) for c in Cflat]
        v_rows = gen[:, 7704:9240].rearrange("p (t c) -> p t c", t=NT)
        recT = qh.rearrange("p (h t) -> p h t", h=HH)
        kdT = [c[:, 0:1024].rearrange("p (b c) -> p b c", b=2) for c in Cflat]
        St_out = kg[0][:, 0:1024].rearrange("p (d h v) -> p d h v", d=2, h=HH)
        St2 = kg[1][:, 0:1024].rearrange("p (d h v) -> p d h v", d=2, h=HH)
        mergedT = hrow[:, :, :].rearrange("p t c -> p (t c)").rearrange("p (j t) -> p j t", j=KC)
        gs = E[0][:, 0:768].rearrange("p (b t) -> p b t", b=2)
        wo_tmp = W[0][:, 0:1024].rearrange("p (b c) -> p b c", b=2)

        off = [0]

        def g(n):
            off[0] += n
            assert off[0] <= 9240
            return gen[:, off[0] - n:off[0]]

        Pm = g(NT * BLK).rearrange("p (t s) -> p t s", t=NT)
        xrow = g(512)
        xT = [g(512).rearrange("p (k s) -> p k s", k=KC) for _ in range(2)]
        gsil, actb = g(256), g(256)
        aT = g(256).rearrange("p (k s) -> p k s", k=4)
        ysb = [g(512) for _ in range(2)]
        Pov = g(NT * BLK).rearrange("p (t s) -> p t s", t=NT)
        xrow_o = g(512)
        xT_o = g(512).rearrange("p (k s) -> p k s", k=KC)
        gsil_o, act_o = g(256), g(256)
        aT_o = g(256).rearrange("p (k s) -> p k s", k=4)
        y_o = g(512)
        pv = g(NT)
        posm = g(NT * NPOS).rearrange("p (t e) -> p t e", t=NT)
        rlog = g(TOK)
        sc, sel, rank, top, oh0, oh1, selm, pos, t48, idxa = [g(NT * NE) for _ in range(10)]
        cmp1, cmp2 = g(192), g(192)
        gsum, grank, gb = g(12), g(12), g(12)
        cnt, novf, ovs, ob = g(16), g(16), g(16), g(16)
        idxf, wsum, wrec = g(6), g(NT), g(NT)
        zeros = S[:, 7936:8192]
        masks32 = S[:, 0:LEV_STEPS * P].bitcast(I32)

        pG = [ctx.enter_context(nc.psum_tensor(f"pG{i}", [P, 512], F32)) for i in range(2)]
        pS = ctx.enter_context(nc.psum_tensor("pS", [P, 2, 512], F32))
        pX = [ctx.enter_context(nc.psum_tensor(f"pX{i}", [P, 512], F32)) for i in range(4)]
        bank = [pG[0][:, :], pG[1][:, :], pS[:, 0, :], pS[:, 1, :]] + [x[:, :] for x in pX]

        landed = [sem(f"landed{s}") for s in range(6)]
        setup_in = sem("setup_in")
        setup_w = sem("setup_w")
        prow_silu = sem("prow_silu")
        prow_T = sem("prow_T")
        cst_ready = sem("cst_ready")
        lb_ready = sem("lb_ready")
        small_in = sem("small_in")
        zeroed = sem("zeroed")
        layer_in = sem("layer_in")
        nw_in = sem("nw_in")
        ctx_in = sem("ctx_in")
        mod_stored = [sem("mod_stored0"), sem("mod_stored1")]
        mod_evac = sem("mod_evac")
        mods_in = sem("mods_in")
        gate_in = sem("gate_in")
        sq_done = sem("sq_done")
        ms_done = sem("ms_done")
        rstd_done = sem("rstd_done")
        h_ready = sem("h_ready")
        hT_made = sem("hT_made")
        hT_v = sem("hT_v")
        hT_a = sem("hT_a")
        group = sem("group")
        qkv_evac = sem("qkv_evac")
        f_sig = sem("f_sig")
        wba_done = sem("wba_done")
        wbh_done = sem("wbh_done")
        wo_evac = sem("wo_evac")
        qk_ms = sem("qk_ms")
        qk_ready = sem("qk_ready")
        qk_T = sem("qk_T")
        qT_ready = sem("qT_ready")
        kT_ready = sem("kT_ready")
        at_scores = sem("at_scores")
        at_max = sem("at_max")
        at_exp = sem("at_exp")
        at_prob = sem("at_prob")
        at_PT = sem("at_PT")
        at_PTv = sem("at_PTv")
        at_PTa = sem("at_PTa")
        at_out = sem("at_out")
        at_outv = sem("at_outv")
        sig_done = sem("sig_done")
        hgq_ready = sem("hgq_ready")
        f_done = sem("f_done")
        ln_done = sem("ln_done")
        C_ready = sem("C_ready")
        vrow_ready = sem("vrow_ready")
        sg_mul = sem("sg_mul")
        sg_ready = sem("sg_ready")
        lv_D = sem("lv_D")
        lv_E = sem("lv_E")
        lv_W = sem("lv_W")
        lv_mm = sem("lv_mm")
        lv_mask = sem("lv_mask")
        fin_D = sem("fin_D")
        fin_E = sem("fin_E")
        fin_W = sem("fin_W")
        kd_T = sem("kd_T")
        kd_Tv = sem("kd_Tv")
        st_mm = sem("st_mm")
        st_ready = sem("st_ready")
        st_stored = sem("st_stored")
        kv_stored = sem("kv_stored")
        o_mm = sem("o_mm")
        o_sq = sem("o_sq")
        o_ms = sem("o_ms")
        o_rstd = sem("o_rstd")
        o_ready = sem("o_ready")
        o_T = sem("o_T")
        rec_ready = sem("rec_ready")
        ga_ready = sem("ga_ready")
        gh_ready = sem("gh_ready")
        merged = sem("merged")
        x_mid = sem("x_mid")
        rt_log = sem("rt_log")
        rt_logv = sem("rt_logv")
        rt_T = sem("rt_T")
        rt_sc = sem("rt_sc")
        rt_sel = sem("rt_sel")
        rt_pos = sem("rt_pos")
        route_ready = sem("route_ready")
        e_P = sem("e_P")
        e_gather = sem("e_gather")
        e_xrow = sem("e_xrow")
        e_xTp = sem("e_xTp")
        e_xT = sem("e_xT")
        e_gate = sem("e_gate")
        e_up = sem("e_up")
        e_silu = sem("e_silu")
        e_act = sem("e_act")
        e_aTp = sem("e_aTp")
        e_aT = sem("e_aT")
        e_down = sem("e_down")
        e_y = sem("e_y")
        e_ydma = [sem("e_ydma0"), sem("e_ydma1")]
        v_pe = sem("v_pe")
        v_dve = sem("v_dve")
        v_act = sem("v_act")
        v_dma = sem("v_dma")
        y_all = sem("y_all")
        yg_in = [sem(f"yg_in{t}") for t in range(NT)]
        x_done = sem("x_done")
        dve_own = sem("dve_own")
        pool_own = sem("pool_own")
        e_own = sem("e_own")
        out_done = sem("out_done")

        block = ctx.enter_context(nc.Block())

        def landed_n(L, name):
            n = UNIT_NO[name]
            s = n % MIX_SLOTS
            return s, 16 * (L * (SLOT_LOADS[s] + NE // 2) + n // MIX_SLOTS + 1)

        def landed_e(L, s, p):
            return 16 * (L * (SLOT_LOADS[s] + NE // 2) + SLOT_LOADS[s]) + (p + 1) * 16

        def gno(L, name):
            return L * NGR + GROUP_NO[name]

        EVAC = {
            "mod": lambda L, i: (mod_evac, 12 * L + i + 1),
            "q": lambda L, i: (qkv_evac, 2 * NT * L + i + 1),
            "kv": lambda L, i: (qkv_evac, 2 * NT * L + NT + i + 1),
            "hq": lambda L, i: (hgq_ready, HH * L + i + 1),
            "ff": lambda L, i: (f_sig, 2 * HH * L + i + 1),
            "fb": lambda L, i: (f_sig, 2 * HH * L + HH + i + 1),
            "i": lambda L, i: (vrow_ready, NT * L + i + 1),
            "g": lambda L, i: (sg_mul, NT * L + i + 1),
            "ga": lambda L, i: (ga_ready, KC * L + i + 1),
            "wba": lambda L, i: (wba_done, KC * L + i + 1),
            "gh": lambda L, i: (gh_ready, KC * L + i + 1),
            "wbh": lambda L, i: (wbh_done, KC * L + i + 1),
            "wo": lambda L, i: (wo_evac, 2 * NT * L + i + 1),
        }

        def bc(ap, shape, axis):
            return ap.unsqueeze(axis).broadcast_to(shape)

        @block.sync
        def _(sp):
            sp.dma_start(prow[0:8, :], a["c_ctx"].rearrange("(k c) -> k c", k=8)).then_inc(setup_in, 16)
            sp.dma_start(prow[8:16, :], a["c"].rearrange("b (k c) -> (b k) c", k=8)).then_inc(setup_in, 16)
            for d, n in enumerate(("hgrn_lb_fwd", "hgrn_lb_bwd")):
                sp.dma_start(prow[16 + 8 * d:24 + 8 * d, :],
                             a[n].rearrange("l (h c) -> (l h) c", h=HH)).then_inc(setup_in, 16)
            sp.dma_start(const[:, :], a["consts"]).then_inc(setup_in, 16)
            ov = sp.alloc_register("sp_further")
            sp.reg_mov(ov, 0)

            def unit(L, name):
                n = UNIT_NO[name]
                s = n % MIX_SLOTS
                kind, i = name
                dst = ring[:, s, :].rearrange("p (k n) -> p k n", k=KC)
                if kind == "mod":
                    src = a["w_mod"][L].rearrange("(k p) n -> p k n", p=P)[:, :, 512 * i:512 * (i + 1)]
                elif kind == "wba" or kind == "wbh":
                    dst = ring[:, s, :].rearrange("p (k n) -> p k n", k=4)
                    src = a["w_br_attn" if kind == "wba" else "w_br_hgrn"][L].rearrange("(k p) n -> p k n", p=P)
                elif kind == "wo":
                    src = a["w_out"][L].rearrange("(k p) n -> p k n", p=P)[:, :, 512 * i:512 * (i + 1)]
                else:
                    width = 256 if kind == "kv" else 512
                    c0 = COL0[name]
                    dst = dst[:, :, 0:width]
                    src = a["w_in"][L].rearrange("(k p) n -> p k n", p=P)[:, :, c0:c0 + width]
                sp.dma_start(dst, src).then_inc(landed[s], 16)

            def expert(L, e, s0, part):
                if part < 2:
                    src = a[("w_exp_gate", "w_exp_up")[part]][L, e, :, :].rearrange("(k p) n -> p k n", p=P)
                    dst = ring[:, s0 + part, :].rearrange("p (k n) -> p k n", k=KC)
                else:
                    src = a["w_exp_down"][L, e, :, :].rearrange("(k p) n -> p k n", p=P)
                    dst = ring[:, s0 + part, :].rearrange("p (k n) -> p k n", k=4)
                return sp.dma_start(dst, src).then_inc(landed[s0 + part], 16)

            def further_done(e):
                sp.reg_add(ov, ov, sp.value_load(nov[0:1, bass.ds(e, 1)], min_val=0, max_val=5))
                sp.wait_ge(v_pe, sp.snap(ov) * 5 + 1)

            for L in range(DEPTH):
                for n, name in enumerate(MIX_UNITS):
                    if n >= MIX_SLOTS:
                        sp.wait_ge(group, gno(L, last_group(MIX_UNITS[n - MIX_SLOTS])) + 1)
                    elif L > 0:
                        if n == 0:
                            sp.wait_ge(e_down, L * NE - 1)
                            further_done(NE - 2)
                        if n == 3:
                            sp.wait_ge(e_down, L * NE)
                            further_done(NE - 1)
                    unit(L, name)
                for part in range(3):
                    last = max(n for n in range(NU) if n % MIX_SLOTS == part)
                    sp.wait_ge(group, gno(L, last_group(MIX_UNITS[last])) + 1)
                    expert(L, 0, 0, part)
                last = max(n for n in range(NU) if n % MIX_SLOTS == 3)
                sp.wait_ge(group, gno(L, last_group(MIX_UNITS[last])) + 1)
                expert(L, 1, 3, 0)
                sp.wait_ge(x_mid, 2 * NT * (L + 1))
                if L == 0:
                    for s in (*e_ydma, v_dma):
                        sp.wait_ge(s, Y0)
                expert(L, 1, 3, 1)
                expert(L, 1, 3, 2)
                sp.wait_ge(route_ready, L + 1)
                with sp.Fori(1, NE // 2) as p:
                    for j in range(2):
                        sp.wait_ge(e_up, p * 2 + (L * NE + j - 1))
                        further_done(p * 2 + (j - 2))
                        expert(L, p * 2 + j, 3 * j, 0)
                        expert(L, p * 2 + j, 3 * j, 1)
                        sp.wait_ge(e_down, p * 2 + (L * NE + j - 1))
                        expert(L, p * 2 + j, 3 * j, 2)
            sp.wait_ge(x_done, NT * (DEPTH - 1) + 1)
            sp.dma_start(y_prompt[0], xs[:, 0, :]).then_inc(out_done, 16)
            for t in range(1, NT):
                sp.wait_ge(x_done, NT * (DEPTH - 1) + t + 1)
                sp.dma_start(y_sample[0, (t - 1) * P:t * P, :], xs[:, t, :]).then_inc(out_done, 16)
            sp.wait_ge(out_done, 16 * NT)
            sp.wait_ge(st_stored, 16 * 2 * DEPTH)
            sp.wait_ge(kv_stored, 16 * 2 * DEPTH)

        @block.gpsimd
        def _(pool):
            own = [0]

            def link(ins):
                own[0] += 1
                ins.then_inc(pool_own, 1)
                pool.wait_ge(pool_own, own[0])

            def load_layer(L):
                if L > 0:
                    pool.wait_ge(group, gno(L - 1, ("mod", 11)) + 1)
                pool.dma_start(brow[0:6 * D // P, :], a["b_mod"][L].rearrange("(r c) -> r c", c=P)).then_inc(layer_in, 16)

            def load_norm(L, which):
                src = a[("norm1_w", "norm2_w")[which]][L:L + 1, :]
                pool.dma_start(nw[:, :], src.broadcast_to([P, D])).then_inc(nw_in, 16)

            def load_mod(L, v, dst, s):
                for cnd in range(2):
                    src = mod_scr[L, cnd:cnd + 1, v * D:(v + 1) * D]
                    pool.dma_start(modb[:, dst, cnd, :], src.broadcast_to([P, D])).then_inc(s, 16)

            def mean_root(s, n, stat0, width, done):
                pool.wait_ge(s, n)
                return pool.tensor_tensor(stat[:, stat0:stat0 + width], stat[:, stat0:stat0 + width],
                                          half[:, 0:width], ALU.pow).then_inc(done, 1)

            pool.wait_ge(zeroed, 1)
            load_layer(0)
            for n, (dst, name, w) in enumerate(((qnw, "q_norm_w", HD), (knw, "k_norm_w", HD), (hnw, "hgrn_norm_w", HK))):
                for L in range(DEPTH):
                    pool.dma_start(dst[:, L, :], a[name][L:L + 1, :].broadcast_to([P, w])).then_inc(small_in, 16)
            pool.dma_start(wr[:, :, :], a["w_router"].rearrange("(k p) e -> p k e", p=P)).then_inc(small_in, 16)
            pool.dma_start(br[:, :], a["b_router"].rearrange("(a e) -> a e", a=1).broadcast_to([P, NE])).then_inc(small_in, 16)
            pool.dma_start(masks32, a["masks"]).then_inc(small_in, 16)
            pool.dma_start(xs[:, 0, :], a["x_prompt"][0]).then_inc(small_in, 16)
            pool.dma_start(xs[:, 1:3, :], a["x_sample"][0].rearrange("(t p) c -> p t c", p=P)).then_inc(small_in, 16)
            for L in range(DEPTH):
                load_norm(L, 0)
                for b in range(2):
                    pool.wait_ge(mod_stored[b], 16 * (12 * L + 4))
                if L > 0:
                    pool.wait_ge(x_done, NT * L)
                load_mod(L, 0, 0, mods_in)
                load_mod(L, 1, 1, mods_in)
                mean_root(ms_done, 2 * L + 1, 0, NT, rstd_done)
                pool.wait_ge(h_ready, 2 * NT * L + NT)
                ck = a["cache_k"][0, L].rearrange("g k d -> k g d")
                for u in range(2):
                    pool.dma_start(Kd[:, 3, :, u, :], ck).then_inc(ctx_in, 16)
                pool.dma_start(Vt[:, 3, :].rearrange("p (g d) -> p g d", g=NKV),
                               a["cache_v"][0, L].rearrange("g k d -> k g d")).then_inc(ctx_in, 16)
                for d, n in enumerate(("state_fwd", "state_bwd")):
                    pool.dma_start(St[:, d, :, :], a[n][0, L].rearrange("h k v -> k h v")).then_inc(ctx_in, 16)
                load_norm(L, 1)
                for n in range(2 * NT):
                    isq, t = n < NT, n % NT
                    heads = NQ if isq else NKV
                    r0 = 16 + 8 * n
                    mean_root(qk_ms, 2 * NT * L + n + 1, r0, heads, pool_own)
                    own[0] += 1
                    pool.wait_ge(pool_own, own[0])
                    x = Q[:, t, :].rearrange("p (h d) -> p h d", h=NQ) if isq else Kd[:, t, :, 0, :]
                    w = (qnw if isq else knw)[:, L, :]
                    link(pool.tensor_tensor(x, x, bc(stat[:, r0:r0 + heads], [P, heads, HD], 2), ALU.mult))
                    last = pool.tensor_tensor(x, x, bc(w, [P, heads, HD], 1), ALU.mult)
                    if t > 0:
                        link(last)
                        cos = const[:, C_COS + HD * (t - 1):C_COS + HD * t]
                        sin = const[:, C_SIN + HD * (t - 1):C_SIN + HD * t].rearrange("p (a b c) -> p a b c", a=2, b=2)
                        A = scratch[:, 0:HD * heads].rearrange("p (h d) -> p h d", h=heads)
                        B = scratch[:, 512:512 + HD * heads].rearrange("p (h d) -> p h d", h=heads)
                        x5 = x.rearrange("p h (a b c) -> p h a b c", a=2, b=2)
                        B5 = B.rearrange("p h (a b c) -> p h a b c", a=2, b=2)
                        pool.tensor_tensor(A, x, bc(cos, [P, heads, HD], 1), ALU.mult)
                        for b in range(2):
                            last = pool.tensor_tensor(B5[:, :, :, b, :], x5[:, :, :, 1 - b, :],
                                                      bc(sin[:, :, b, :], [P, heads, 2, 16], 1), ALU.mult)
                        link(last)
                        last = pool.tensor_tensor(x, A, B, ALU.add)
                    if not isq:
                        link(last)
                        last = pool.tensor_scalar(Kd[:, t, :, 1, :], x, 1.0, None, ALU.mult)
                    last.then_inc(qk_ready, 1)
                for t in range(NT):
                    pool.wait_ge(sg_mul, NT * L + t + 1)
                    s4 = sg[:, t, :].rearrange("p (h v) -> p h v", h=HH)
                    pool.tensor_tensor(s4, s4, bc(hnw[:, L, :], [P, HH, HK], 1), ALU.mult).then_inc(sg_ready, 1)
                pool.wait_ge(at_outv, ATT_STEPS * (L + 1))
                for s in range(2 * NLEV):
                    m, d = 64 >> (s // 2), s % 2
                    pool.wait_ge(C_ready, 2 * L + d + 1)
                    if s >= 2:
                        pool.wait_ge(lv_W, LEV_STEPS * L + s - 1)
                    base = Cs[d][:, :, 1 - d:129 - d].rearrange("p s (b u m) -> p s b u m", u=2, m=m)
                    mid = Cs[d][:, :, m:m + 128 - 2 * m + 1:2 * m] if m < 64 else Cs[d][:, :, 64:65]
                    mid = mid.unsqueeze(3).broadcast_to([P, SEG, 64 // m, m])
                    out = E[d].rearrange("p (s b u m) -> p s b u m", s=SEG, u=2, m=m)
                    pool.tensor_tensor(out[:, :, :, 0, :], mid, base[:, :, :, 0, :], ALU.subtract)
                    pool.tensor_tensor(out[:, :, :, 1, :], base[:, :, :, 1, :], mid, ALU.subtract).then_inc(lv_D, 1)
                pool.wait_ge(lv_W, LEV_STEPS * (L + 1))
                for d, dst in ((0, E[0]), (1, W[0])):
                    if d == 1:
                        pool.wait_ge(lv_mm, LEV_TILES * (L + 1))
                    end = Cs[d][:, :, 128:129].broadcast_to([P, SEG, P])
                    pool.tensor_tensor(dst.rearrange("p (s t) -> p s t", s=SEG), end, Cs[d][:, :, 1 - d:129 - d],
                                       ALU.subtract).then_inc(fin_D, 1)
                for t in range(NT):
                    mean_root(o_ms, NT * L + t + 1, 64 + 4 * t, HH, o_rstd)
                for b in range(2):
                    pool.wait_ge(mod_stored[b], 16 * 12 * (L + 1))
                load_mod(L, 2, 2, gate_in)
                pool.wait_ge(group, gno(L, ("wba", KC - 1)) + 1)
                pool.wait_ge(o_mm, NT * (L + 1))
                pool.wait_ge(st_ready, 4 * (L + 1))
                load_mod(L, 3, 0, mods_in)
                load_mod(L, 4, 1, mods_in)
                mean_root(ms_done, 2 * L + 2, 0, NT, rstd_done)
                pool.wait_ge(x_mid, 2 * NT * (L + 1))
                load_mod(L, 5, 2, gate_in)
                if L + 1 < DEPTH:
                    load_layer(L + 1)
                pool.wait_ge(y_all, L + 1)
                for t in range(NT):
                    for c in range(2):
                        dst = modb[:, t, c, :] if t < 2 else hrow[:, c, :]
                        pool.indirect_dma_start(dst, None, y_scr[:, :],
                                                bass.IndirectOffsetOnAxis(ap=idx[:, c, t:t + 1], axis=0)
                                                ).then_inc(yg_in[t], 16)

        @block.scalar
        def _(act):
            def sync_group(L, name):
                act.wait_ge(group, gno(L, name) + 1)
                return bank[gno(L, name) % 2]

            act.sem_inc(e_silu, 1)
            act.sem_inc(e_y, 1)
            act.wait_ge(zeroed, 1)
            for i, r in enumerate(range(NE * BLK, YROWS, P)):
                act.dma_start(y_scr[r:r + P, :].rearrange("p (a c) -> p a c", a=4),
                              bc(zeros, [P, 4, 256], 1)).then_inc((*e_ydma, v_dma)[i % 3], 16)
            act.wait_ge(setup_in, 16 * 5)
            act.activation(prow[0:16, :], prow[0:16, :], ACT.Silu).then_inc(prow_silu, 1)
            act.wait_ge(lb_ready, 1)
            act.activation(lbe[:, 1:3, :], lbe[:, 1:3, :], ACT.Exp).then_inc(lb_ready, 1)
            further = act.alloc_register("act_further")
            further_l = act.alloc_register("act_further_layer")
            act.reg_mov(further, 0)

            def mod_store(L, m):
                ps = sync_group(L, ("mod", m))
                act.wait_ge(mod_stored[m % 2], 16 * (12 * L + 2 * (m // 2)))
                act.copy(mstage[:, m % 2, :], ps[:, 0:P]).then_inc(mod_evac, 1)
                act.wait_ge(mod_evac, 12 * L + m + 1)
                for cnd in range(2):
                    dst = mod_scr[L, cnd, 512 * m:512 * (m + 1)].rearrange("(j c) -> j c", c=P)
                    act.dma_start(dst, mstage[16 * cnd:16 * cnd + 97:32, m % 2, :]).then_inc(mod_stored[m % 2], 16)

            def norm(L, which):
                if which == 0:
                    if L > 0:
                        act.wait_ge(x_done, NT * L)
                else:
                    act.wait_ge(x_mid, 2 * NT * (L + 1))
                for t in range(NT):
                    act.activation(hrow[:, t, :], xs[:, t, :], ACT.Square,
                                   accum_out=stat[:, t:t + 1]).then_inc(sq_done, 1)
                for t in range(NT):
                    act.wait_ge(hT_made, 2 * NT * (2 * L + which) + 2 * t + 2)
                    act.copy(hT[:, 4:8, t * P:(t + 1) * P],
                             bank[3 + 2 * t].rearrange("p (k t) -> p k t", k=4)).then_inc(hT_a, 1)

            def att(L, k):
                if k < ATT_STEPS:
                    nk = P if k % NT == 0 else 3 * P
                    c0 = 80 + 8 * (k % 2)
                    act.wait_ge(at_max, ATT_STEPS * L + k + 1)
                    if k >= 2:
                        act.wait_ge(at_PT, ATT_STEPS * L + k - 1)
                    for u in range(2):
                        act.activation(prob[:, k % 2, u, 0:nk], bank[2 + u][:, 0:nk], ACT.Exp,
                                       bias=stat[:, c0 + 2 + u:c0 + 3 + u], scale=float(HD) ** -0.5,
                                       accum_out=stat[:, c0 + 4 + u:c0 + 5 + u]).then_inc(at_exp, 1)
                if 1 <= k <= ATT_STEPS:
                    nk = P if (k - 1) % NT == 0 else 3 * P
                    act.wait_ge(at_PT, ATT_STEPS * L + k)
                    if k >= 2:
                        act.wait_ge(at_out, ATT_STEPS * L + k - 1)
                    act.copy(PT[:, 1, 0:nk], bank[5][:, 0:nk]).then_inc(at_PTa, 1)

            def lev(L, s):
                if s < 2 * NLEV:
                    act.wait_ge(lv_D, 2 * NLEV * L + s + 1)
                    act.activation(E[s % 2], E[s % 2], ACT.Exp).then_inc(lv_E, 1)

            for L in range(DEPTH):
                for m in range(4):
                    mod_store(L, m)
                if L == 0:
                    act.wait_ge(small_in, SMALL_LOADS)
                norm(L, 0)
                for h in range(HH - 1):
                    sync_group(L, ("hq", h))
                    act.activation(qh[:, h * TOK:(h + 1) * TOK], bank[gno(L, ("hq", h)) % 2][:, 0:TOK],
                                   ACT.Sigmoid).then_inc(sig_done, 1)
                act.wait_ge(qk_T, 5 * (L + 1))
                for gk in range(NKV):
                    act.copy(kT[:, gk, :], bank[5 + gk]).then_inc(kT_ready, 1)
                act.wait_ge(qk_ready, 2 * NT * L + NT + 1)
                act.dma_start(new_k[0, L].rearrange("g k d -> k g d"), Kd[:, 0, :, 0, :]).then_inc(kv_stored, 16)
                act.wait_ge(qkv_evac, 2 * NT * L + NT + 1)
                act.dma_start(new_v[0, L].rearrange("g k d -> k g d"),
                              Vt[:, 0, :].rearrange("p (g d) -> p g d", g=NKV)).then_inc(kv_stored, 16)
                ps = sync_group(L, ("hq", HH - 1))
                act.activation(qh[:, (HH - 1) * TOK:HH * TOK], ps[:, 0:TOK], ACT.Sigmoid).then_inc(sig_done, 1)
                att(L, 0)
                if L > 0:
                    act.wait_ge(st_stored, 16 * 2 * L)
                for d, kind in enumerate(("ff", "fb")):
                    for h in range(HH):
                        ps = sync_group(L, (kind, h))
                        act.activation(kg[d][:, h * TOK:(h + 1) * TOK], ps[:, 0:TOK],
                                       ACT.Sigmoid).then_inc(f_sig, 1)
                        att(L, ATT_AT[(kind, h)])
                    act.wait_ge(f_done, 2 * HH * L + HH * (d + 1))
                    if d == 0:
                        act.wait_ge(qk_ready, 2 * NT * (L + 1))
                    else:
                        act.wait_ge(C_ready, 2 * L + 1)
                    act.activation(scratch, kg[d], ACT.Ln).then_inc(ln_done, 1)
                for t in range(NT):
                    ps = sync_group(L, ("i", t))
                    act.copy(v_rows[:, t, :], ps).then_inc(vrow_ready, 1)
                    att(L, ATT_AT[("i", t)])
                for t in range(NT):
                    ps = sync_group(L, ("g", t))
                    act.activation(sg[:, t, :], ps, ACT.Sigmoid).then_inc(sig_done, 1)
                    if ("g", t) in ATT_AT:
                        att(L, ATT_AT[("g", t)])
                lev(L, 0)
                lev(L, 1)
                for j in range(KC):
                    ps = sync_group(L, ("ga", j))
                    act.activation(mergedT[:, j, :], ps[:, 0:TOK], ACT.Sigmoid).then_inc(ga_ready, 1)
                    lev(L, LEV_AT[("ga", j)] + 2)
                for m in range(4, 12):
                    mod_store(L, m)
                    if ("mod", m) in LEV_AT:
                        lev(L, LEV_AT[("mod", m)] + 2)
                act.wait_ge(lv_mm, LEV_TILES * L + NT * 14)
                act.activation(W[1].rearrange("p (s t) -> p s t", s=SEG), Cs[0][:, :, 1:129], ACT.Exp)
                for d in range(2):
                    ins = act.activation(dec[:, d, :], Cs[d][:, :, 128], ACT.Exp)
                ins.then_inc(fin_E, 1)
                act.wait_ge(fin_D, 2 * L + 1)
                act.activation(E[0], E[0], ACT.Exp).then_inc(fin_E, 1)
                act.wait_ge(fin_D, 2 * L + 2)
                act.activation(W[0], W[0], ACT.Exp).then_inc(fin_E, 1)
                act.wait_ge(lv_W, LEV_STEPS * (L + 1))
                act.activation(E[1].rearrange("p (s t) -> p s t", s=SEG), Cs[1][:, :, 0:128], ACT.Exp).then_inc(fin_E, 1)
                act.wait_ge(st_ready, 4 * L + 2)
                for d in range(2):
                    dst = (new_sf, new_sb)[d][0, L].rearrange("h k v -> k h v")
                    act.dma_start(dst, St_out[:, d, :, :]).then_inc(st_stored, 16)
                for t in range(NT):
                    act.wait_ge(o_mm, NT * L + t + 1)
                    act.activation(E[0][:, t * 512:(t + 1) * 512], bank[O_BANK[t]], ACT.Square).then_inc(o_sq, 1)
                for t in range(NT):
                    act.wait_ge(o_T, NT * L + t + 1)
                    act.copy(recT[:, :, t * P:(t + 1) * P],
                             bank[3 + t].rearrange("p (h t) -> p h t", h=HH)).then_inc(rec_ready, 1)
                for j in range(KC):
                    ps = sync_group(L, ("gh", j))
                    if j >= 2:
                        act.wait_ge(merged, KC * L + j - 1)
                    act.activation(gs[:, j % 2, :], ps[:, 0:TOK], ACT.Sigmoid).then_inc(gh_ready, 1)
                norm(L, 1)
                act.wait_ge(rt_T, L + 1)
                act.activation(sc, bank[3][:, 0:NT * NE], ACT.Sigmoid).then_inc(rt_sc, 1)
                act.wait_ge(route_ready, L + 1)
                act.reg_mov(further_l, 0)
                with act.Fori(0, NE // 2) as p:
                    for j in range(2):
                        n = p * 2 + (L * NE + j)
                        act.wait_ge(e_gate, n + 1)
                        act.wait_ge(e_act, n + 1)
                        act.activation(gsil, bank[2][:, 0:256], ACT.Silu).then_inc(e_silu, 1)
                        act.wait_ge(e_down, n + 1)
                        act.wait_ge(e_ydma[j], (p + L * NE // 2) * 32 + Y0)
                        act.copy(ysb[j], bank[1]).then_inc(e_y, 1)
                        act.wait_ge(e_y, n + 2)
                        for hf in range(2):
                            act.dma_start(y_scr[bass.ds(p * (2 * BLK) + j * BLK, BLK), 512 * hf:512 * (hf + 1)],
                                          ysb[j][BLK * hf:BLK * (hf + 1), :]).then_inc(e_ydma[j], 16)
                        more = act.value_load(nov[0:1, bass.ds(p * 2 + j, 1)], min_val=0, max_val=5)
                        with act.If(more > 0):
                            with act.Fori(0, more):
                                b = act.snap(further)
                                act.wait_ge(v_pe, b * 5 + 4)
                                act.activation(gsil_o, bank[6][:, 0:256], ACT.Silu).then_inc(v_act, 1)
                                act.wait_ge(v_dve, b * 7 + 7)
                                row = act.snap(further_l, min_val=0, max_val=MAX_EXTRA - 1) * BLK + NE * BLK
                                for hf in range(2):
                                    act.dma_start(y_scr[bass.ds(row, BLK), 512 * hf:512 * (hf + 1)],
                                                  y_o[BLK * hf:BLK * (hf + 1), :]).then_inc(v_dma, 16)
                                act.reg_add(further, further, 1)
                                act.reg_add(further_l, further_l, 1)
                for j in range(2):
                    act.wait_ge(e_ydma[j], 32 * (NE // 2) * (L + 1) + Y0)
                act.wait_ge(v_dma, act.snap(further) * 32 + Y0)
                act.sem_inc(y_all, 1)

        @block.vector
        def _(dve):
            own = [0]

            def link(ins):
                own[0] += 1
                ins.then_inc(dve_own, 1)
                dve.wait_ge(dve_own, own[0])

            def sync_group(L, name):
                dve.wait_ge(group, gno(L, name) + 1)
                return bank[gno(L, name) % 2]

            def seg4(ap):
                return ap.rearrange("p (s t) -> p s t", s=SEG)

            dve.sem_inc(e_act, 1)
            dve.memset(half[:, :], -0.5)
            dve.memset(brow[:, :], 0.0)
            dve.memset(zeros, 0.0).then_inc(zeroed, 1)
            dve.wait_ge(prow_T, 1)
            for cnd in range(2):
                ins = dve.tensor_copy(cst[:, :, cnd, :], bc(bank[2][:, 8 * cnd:8 * cnd + 8], [P, KC, 16], 2))
            ins.then_inc(cst_ready, 1)
            link(dve.tensor_copy(lraw[:, :], bank[2][:, 16:32]))
            lr = lraw[:, :].rearrange("p (d l h) -> p l d h", d=2, l=DEPTH)
            lb4 = lbe[:, :, :].rearrange("p n (d h) -> p n d h", d=2)
            link(dve.tensor_tensor(lb4[:, 0], lr[:, 0], lr[:, 1], ALU.max))
            for l in range(DEPTH):
                ins = dve.tensor_tensor(lb4[:, 1 + l], lr[:, l], lb4[:, 0], ALU.subtract)
            ins.then_inc(lb_ready, 1)
            dve.wait_ge(lb_ready, 2)
            link(dve.tensor_tensor(lbe[:, 0, :], lbe[:, 1, :], lbe[:, 2, :], ALU.add))
            link(dve.reciprocal(lbe[:, 3, :], lbe[:, 0, :]))
            link(dve.tensor_tensor(lbe[:, 1, :], lbe[:, 1, :], lbe[:, 3, :], ALU.mult))
            link(dve.tensor_tensor(lbe[:, 2, :], lbe[:, 2, :], lbe[:, 3, :], ALU.mult))
            link(dve.tensor_tensor(lbe[:, 0, :], lbe[:, 1, :], lbe[:, 2, :], ALU.add))
            dve.tensor_tensor(lbT[:, 0].rearrange("p d h -> p (d h)"), lbe[:, 1, :], lbe[:, 1, :], ALU.subtract)
            link(dve.tensor_tensor(lbT[:, 1].rearrange("p d h -> p (d h)"), lbe[:, 0, :], lbe[:, 1, :], ALU.subtract))
            link(dve.tensor_scalar(omT[:, :, :, :].rearrange("p l d h -> p (l d h)"),
                                   lbT[:, :, :, :].rearrange("p l d h -> p (l d h)"), -1.0, 1.0, ALU.mult, ALU.add))

            def norm(L, which):
                n = 2 * L + which
                dve.wait_ge(mods_in, 16 * 4 * (n + 1))
                dve.wait_ge(nw_in, 16 * (n + 1))
                for cnd in range(2):
                    ins = dve.scalar_tensor_tensor(modb[:, 1, cnd, :], modb[:, 1, cnd, :], 1.0, nw[:, :],
                                                   ALU.add, ALU.mult)
                link(ins)
                dve.wait_ge(sq_done, NT * (n + 1))
                dve.tensor_scalar(stat[:, 0:NT], stat[:, 0:NT], 1.0 / D, EPS, ALU.mult, ALU.add).then_inc(ms_done, 1)
                dve.wait_ge(rstd_done, n + 1)
                for t in range(NT):
                    cnd = min(t, 1)
                    link(dve.scalar_tensor_tensor(hrow[:, t, :], xs[:, t, :], stat[:, t:t + 1], modb[:, 1, cnd, :],
                                                  ALU.mult, ALU.mult))
                    dve.tensor_tensor(hrow[:, t, :], hrow[:, t, :], modb[:, 0, cnd, :], ALU.add).then_inc(h_ready, 1)
                for t in range(NT):
                    dve.wait_ge(hT_made, 2 * NT * n + 2 * t + 1)
                    dve.tensor_copy(hT[:, 0:4, t * P:(t + 1) * P],
                                    bank[2 + 2 * t].rearrange("p (k t) -> p k t", k=4)).then_inc(hT_v, 1)

            def att(L, k):
                if k < ATT_STEPS:
                    nk = P if k % NT == 0 else 3 * P
                    c0 = 80 + 8 * (k % 2)
                    dve.wait_ge(at_scores, ATT_STEPS * L + k + 1)
                    link(dve.tensor_reduce(stat[:, c0:c0 + 2], pS[:, :, 0:nk], AX.X, ALU.max))
                    dve.tensor_scalar(stat[:, c0 + 2:c0 + 4], stat[:, c0:c0 + 2], -float(HD) ** -0.5, None,
                                      ALU.mult).then_inc(at_max, 1)
                    dve.wait_ge(at_exp, 2 * (ATT_STEPS * L + k + 1))
                    link(dve.reciprocal(stat[:, c0 + 6:c0 + 8], stat[:, c0 + 4:c0 + 6]))
                    for u in range(2):
                        x = prob[:, k % 2, u, 0:nk]
                        ins = dve.tensor_scalar(x, x, stat[:, c0 + 6 + u:c0 + 7 + u], None, ALU.mult)
                    ins.then_inc(at_prob, 1)
                if 1 <= k <= ATT_STEPS:
                    nk = P if (k - 1) % NT == 0 else 3 * P
                    dve.wait_ge(at_PT, ATT_STEPS * L + k)
                    if k >= 2:
                        dve.wait_ge(at_out, ATT_STEPS * L + k - 1)
                    dve.tensor_copy(PT[:, 0, 0:nk], bank[4][:, 0:nk]).then_inc(at_PTv, 1)
                if k >= 2:
                    r, t = (k - 2) // NT, (k - 2) % NT
                    dve.wait_ge(at_out, ATT_STEPS * L + k - 1)
                    dve.tensor_copy(attnT[:, r, t * P:(t + 1) * P], bank[6][:, 0:P]).then_inc(at_outv, 1)

            def lev(L, s):
                lev_mask(L, s - 2)
                if s < LEV_STEPS:
                    if s >= 2:
                        dve.wait_ge(lv_mm, LEV_TILES * L + NT * (s - 1))
                    if s < 2 * NLEV:
                        m, d = 64 >> (s // 2), s % 2
                        dve.wait_ge(lv_E, 2 * NLEV * L + s + 1)
                        Wv, Ev, qv, kv = (x.rearrange("p (s b u m) -> p s b u m", s=SEG, u=2, m=m)
                                          for x in (W[d], E[d], qh, kg[d]))
                        for u in range(2):
                            src = kv if u == d else qv
                            ins = dve.tensor_tensor(Wv[:, :, :, u, :], src[:, :, :, u, :], Ev[:, :, :, u, :], ALU.mult)
                    else:
                        ins = dve.tensor_tensor(W[0], kg[0], kg[1], ALU.add)
                    ins.then_inc(lv_W, 1)

            def lev_mask(L, s):
                if s >= 0:
                    for t in range(NT):
                        u = NT * s + t
                        dve.wait_ge(lv_mm, LEV_TILES * L + u + 1)
                        if u >= NT:
                            dve.wait_ge(lv_mask, LEV_TILES * L + u - 2)
                        A4 = AT.rearrange("p (h t) c -> p h t c", h=HH)[:, :, t, :]
                        dve.copy_predicated(A4, bc(masks[:, s, :], [P, HH, P], 1),
                                            bank[2 + u % 4].rearrange("p (h t) -> p h t", h=HH)).then_inc(lv_mask, 1)

            def wba(L, j):
                ps = sync_group(L, ("wba", j))
                dve.wait_ge(ga_ready, KC * (L + 1))
                dve.tensor_tensor(mergedT[:, j, :], ps[:, 0:TOK], mergedT[:, j, :], ALU.mult).then_inc(wba_done, 1)

            def fin(L, i, dst, src):
                dve.wait_ge(fin_E, 4 * L + i + 1)
                dve.tensor_tensor(dst, dst, src, ALU.mult).then_inc(fin_W, 1)

            def kd_evac(L, i):
                dve.wait_ge(kd_T, 4 * L + i + 1)
                dve.tensor_copy(kdT[i // 2][:, i % 2, :], bank[2 + i]).then_inc(kd_Tv, 1)

            dve.wait_ge(small_in, SMALL_LOADS)
            link(dve.tensor_copy(masks[:, :, :].rearrange("p s t -> p (s t)"), masks32))
            further = dve.alloc_register("dve_further")
            dve.reg_mov(further, 0)

            for L in range(DEPTH):
                norm(L, 0)
                for d in range(2):
                    dve.memset(Cs[d][:, :, 0:1], 0.0)
                for n in range(2 * NT):
                    isq, t = n < NT, n % NT
                    heads = NQ if isq else NKV
                    ps = sync_group(L, ("q" if isq else "kv", t))
                    x = Q[:, t, :].rearrange("p (h d) -> p h d", h=NQ) if isq else Kd[:, t, :, 0, :]
                    ins = dve.tensor_copy(x, ps[:, 0:heads * HD].rearrange("p (h d) -> p h d", h=heads))
                    if not isq:
                        ins = dve.tensor_copy(Vt[:, t, :], ps[:, P:2 * P])
                    ins.then_inc(qkv_evac, 1)
                    dve.wait_ge(qkv_evac, 2 * NT * L + n + 1)
                    sq = scratch[:, 1024:1024 + heads * HD].rearrange("p (h d) -> p h d", h=heads)
                    link(dve.tensor_tensor(sq, x, x, ALU.mult))
                    ms = stat[:, 16 + 8 * n:16 + 8 * n + heads]
                    link(dve.tensor_reduce(ms, sq, AX.X, ALU.add))
                    dve.tensor_scalar(ms, ms, 1.0 / HD, EPS, ALU.mult, ALU.add).then_inc(qk_ms, 1)

                def hq(h):
                    ps = sync_group(L, ("hq", h))
                    dve.wait_ge(sig_done, (HH + NT) * L + h + 1)
                    x = qh[:, h * TOK:(h + 1) * TOK]
                    dve.scalar_tensor_tensor(x, ps[:, 0:TOK], float(HK) ** -0.5, x, ALU.mult,
                                             ALU.mult).then_inc(hgq_ready, 1)

                for h in range(HH - 1):
                    hq(h)
                for t in range(NT):
                    dve.wait_ge(qk_T, 5 * L + t + 1)
                    dve.tensor_copy(qTa[:, :, t * P:(t + 1) * P],
                                    bank[2 + t].rearrange("p (r t) -> p r t", r=4)).then_inc(qT_ready, 1)
                hq(HH - 1)
                att(L, 0)
                for d, kind in enumerate(("ff", "fb")):
                    for h in range(HH):
                        dve.wait_ge(f_sig, 2 * HH * L + HH * d + h + 1)
                        x = kg[d][:, h * TOK:(h + 1) * TOK]
                        dve.tensor_scalar(x, x, omT[:, L, d, h:h + 1], lbT[:, L, d, h:h + 1], ALU.mult,
                                          ALU.add).then_inc(f_done, 1)
                        att(L, ATT_AT[(kind, h)])
                    dve.wait_ge(ln_done, 2 * L + d + 1)
                    for s in range(SEG):
                        dve.tensor_tensor_scan(Cs[d][:, s, 1:129], ones, scratch[:, s * P:(s + 1) * P], 0.0,
                                               ALU.mult, ALU.add)
                    dve.tensor_scalar(kg[d], kg[d], -1.0, 1.0, ALU.mult, ALU.add).then_inc(C_ready, 1)
                for t in range(NT):
                    att(L, ATT_AT[("i", t)])
                for t in range(NT):
                    ps = sync_group(L, ("g", t))
                    dve.wait_ge(sig_done, (HH + NT) * L + HH + t + 1)
                    dve.tensor_tensor(sg[:, t, :], ps, sg[:, t, :], ALU.mult).then_inc(sg_mul, 1)
                    if ("g", t) in ATT_AT:
                        att(L, ATT_AT[("g", t)])
                dve.wait_ge(kv_stored, 16 * 2 * (L + 1))
                for s in range(LEV_STEPS + 2):
                    lev(L, s)
                fin(L, 0, W[1], qh)
                fin(L, 1, E[0], kg[0])
                wba(L, 0)
                fin(L, 2, W[0], qh)
                fin(L, 3, E[1], kg[1])
                kd_evac(L, 0)
                kd_evac(L, 1)
                wba(L, 1)
                kd_evac(L, 2)
                kd_evac(L, 3)
                wba(L, 2)
                for i, (d, b) in enumerate(((0, 2), (1, 4))):
                    dve.wait_ge(st_mm, 4 * L + i + 1)
                    dve.tensor_copy(St_out[:, d, :, :], bank[b].rearrange("p (h v) -> p h v", h=HH)).then_inc(st_ready, 1)
                dve.wait_ge(ctx_in, 16 * 5 * (L + 1))
                for d, b, t in ((0, 3, 1), (1, 5, 2)):
                    dve.wait_ge(st_mm, 4 * L + 3 + d)
                    for h in range(HH):
                        ins = dve.scalar_tensor_tensor(St2[:, d, h, :], St[:, d, h, :], dec[:, d, h * NT + t:h * NT + t + 1],
                                                       bank[b][:, h * P:(h + 1) * P], ALU.mult, ALU.add)
                    ins.then_inc(st_ready, 1)
                wba(L, 3)
                for t in range(NT):
                    dve.wait_ge(o_sq, NT * L + t + 1)
                    ms = stat[:, 64 + 4 * t:68 + 4 * t]
                    link(dve.tensor_reduce(ms, E[0][:, t * 512:(t + 1) * 512].rearrange("p (h v) -> p h v", h=HH),
                                           AX.X, ALU.add))
                    dve.tensor_scalar(ms, ms, 1.0 / HK, EPS, ALU.mult, ALU.add).then_inc(o_ms, 1)
                wba(L, 4)
                wba(L, 5)
                for t in range(NT):
                    dve.wait_ge(o_rstd, NT * L + t + 1)
                    dve.wait_ge(sg_ready, NT * L + t + 1)
                    o4 = orow[:, t, :].rearrange("p (h v) -> p h v", h=HH)
                    link(dve.tensor_tensor(o4, bank[O_BANK[t]].rearrange("p (h v) -> p h v", h=HH),
                                           bc(stat[:, 64 + 4 * t:68 + 4 * t], [P, HH, HK], 2), ALU.mult))
                    dve.tensor_tensor(orow[:, t, :], orow[:, t, :], sg[:, t, :], ALU.mult).then_inc(o_ready, 1)
                wba(L, 6)
                wba(L, 7)
                for j in range(KC):
                    ps = sync_group(L, ("wbh", j))
                    dve.wait_ge(gh_ready, KC * L + j + 1)
                    dve.tensor_tensor(gs[:, j % 2, :], ps[:, 0:TOK], gs[:, j % 2, :], ALU.mult).then_inc(wbh_done, 1)
                    dve.wait_ge(wbh_done, KC * L + j + 1)
                    dve.tensor_tensor(mergedT[:, j, :], mergedT[:, j, :], gs[:, j % 2, :], ALU.add).then_inc(merged, 1)
                dve.wait_ge(gate_in, 16 * (4 * L + 2))
                for n in range(2 * NT):
                    i, t = n // NT, n % NT
                    ps = sync_group(L, ("wo", n))
                    dve.tensor_tensor(wo_tmp[:, n % 2, :], ps, modb[:, 2, min(t, 1), 512 * i:512 * (i + 1)],
                                      ALU.mult).then_inc(wo_evac, 1)
                    dve.wait_ge(wo_evac, 2 * NT * L + n + 1)
                    x = xs[:, t, 512 * i:512 * (i + 1)]
                    dve.tensor_tensor(x, x, wo_tmp[:, n % 2, :], ALU.add).then_inc(x_mid, 1)
                norm(L, 1)
                dve.wait_ge(st_stored, 16 * 2 * (L + 1))
                dve.wait_ge(rt_log, L + 1)
                dve.tensor_copy(rlog[0:NE, :], bank[2][0:NE, 0:TOK]).then_inc(rt_logv, 1)
                dve.wait_ge(rt_sc, L + 1)

                def t3(x):
                    return x.rearrange("p (t e) -> p t e", t=NT)

                def ranks(out, x, n):
                    xv = x.rearrange("p (n i) -> p n i", i=4)
                    xi = xv.unsqueeze(2).broadcast_to([P, n, 4, 4])
                    xj = xv.unsqueeze(3).broadcast_to([P, n, 4, 4])
                    a4 = cmp1[:, 0:16 * n].rearrange("p (n j i) -> p n j i", j=4, i=4)
                    b4 = cmp2[:, 0:16 * n].rearrange("p (n j i) -> p n j i", j=4, i=4)
                    before = const[:, C_BEFORE:C_BEFORE + 16]
                    dve.tensor_tensor(a4, xi, xj, ALU.is_gt)
                    link(dve.tensor_tensor(b4, xi, xj, ALU.is_equal))
                    b3 = cmp2[:, 0:16 * n].rearrange("p (n c) -> p n c", c=16)
                    link(dve.tensor_tensor(b3, b3, bc(before, [P, n, 16], 1), ALU.mult))
                    link(dve.tensor_tensor(cmp1[:, 0:16 * n], cmp1[:, 0:16 * n], cmp2[:, 0:16 * n], ALU.add))
                    link(dve.tensor_reduce(out.rearrange("p (n j) -> p n j", j=4), a4, AX.X, ALU.add))

                link(dve.tensor_tensor(t3(sel), t3(sc), bc(br[:, :], [P, NT, NE], 1), ALU.add))
                ranks(rank, sel, NT * NG)
                link(dve.scalar_tensor_tensor(top, rank, 1.5, sel, ALU.is_lt, ALU.mult))
                link(dve.tensor_reduce(gsum, top.rearrange("p (n j) -> p n j", j=4), AX.X, ALU.add))
                ranks(grank, gsum, NT)
                link(dve.tensor_scalar(gb, grank, 0.5, None, ALU.is_lt))
                gbb = bc(gb, [P, NT * NG, 4], 2)
                for val, oh in ((0.0, oh0), (1.0, oh1)):
                    ins = dve.scalar_tensor_tensor(oh.rearrange("p (n j) -> p n j", j=4),
                                                   rank.rearrange("p (n j) -> p n j", j=4), val, gbb,
                                                   ALU.is_equal, ALU.mult)
                link(ins)
                dve.tensor_tensor(selm, oh0, oh1, ALU.add).then_inc(rt_sel, 1)
                dve.wait_ge(rt_sel, L + 1)
                link(dve.tensor_tensor(t48, sc, selm, ALU.mult))
                link(dve.tensor_reduce(wsum, t3(t48), AX.X, ALU.add))
                link(dve.reciprocal(wrec, wsum))
                for c, oh in enumerate((oh0, oh1)):
                    link(dve.tensor_tensor(t48, sc, oh, ALU.mult))
                    link(dve.tensor_reduce(wgt[:, c, :], t3(t48), AX.X, ALU.add))
                    link(dve.tensor_tensor(wgt[:, c, :], wgt[:, c, :], wrec, ALU.mult))
                dve.wait_ge(rt_pos, L + 1)
                dve.tensor_copy(pos, bank[4][:, 0:NT * NE])
                link(dve.tensor_copy(cnt, bank[4][:, NT * NE:NT * NE + NE]))
                dve.memset(posm, FAR)
                link(dve.tensor_scalar(t48, selm, -FAR, FAR, ALU.mult, ALU.add))
                link(dve.tensor_tensor(posm[:, :, 0:NE], t3(pos), t3(t48), ALU.add))
                link(dve.tensor_scalar(novf, cnt, float(BLK), None, ALU.is_gt))
                for b in range(2, TOK // BLK):
                    link(dve.scalar_tensor_tensor(novf, cnt, float(BLK * b), novf, ALU.is_gt, ALU.add))
                dve.tensor_copy(nov[:, :], novf[0:1, :])
                link(dve.tensor_tensor_scan(ovs, ones[:, 0:NE], novf, 0.0, ALU.mult, ALU.add))
                link(dve.tensor_tensor(ovs, ovs, novf, ALU.subtract))
                link(dve.scalar_tensor_tensor(ob, ovs, float(BLK), const[:, C_OB:C_OB + NE], ALU.mult, ALU.add))
                link(dve.scalar_tensor_tensor(t3(idxa), t3(pos), float(BLK), bc(ob, [P, NT, NE], 1),
                                              ALU.is_ge, ALU.mult))
                link(dve.tensor_tensor(idxa, idxa, pos, ALU.add))
                link(dve.tensor_tensor(t3(idxa), t3(idxa), bc(const[:, C_E64:C_E64 + NE], [P, NT, NE], 1), ALU.add))
                for c, oh in enumerate((oh0, oh1)):
                    link(dve.tensor_tensor(t48, idxa, oh, ALU.mult))
                    link(dve.tensor_reduce(idxf[:, NT * c:NT * (c + 1)], t3(t48), AX.X, ALU.add))
                dve.tensor_copy(idx[:, :, :].rearrange("p c t -> p (c t)"), idxf).then_inc(route_ready, 1)
                dve.wait_ge(route_ready, L + 1)

                def one_hot(dst, where, done):
                    for t in range(NT):
                        ins = dve.tensor_scalar(dst[:, t, :], iota, where[:, t:t + 1] if len(where.shape) == 2
                                                else where[:, t, :], None, ALU.is_equal)
                    ins.then_inc(done, 1)

                def xT_view(dst):
                    return dst.rearrange("p (a c) s -> p c a s", a=2)

                def xT_src(b):
                    return bank[b].rearrange("p (c a s) -> p c a s", c=4, a=2)

                def aT_dst(dst):
                    return dst.rearrange("p (a c) s -> p c a s", a=2)

                def aT_src(b):
                    return bank[b][:, 0:256].rearrange("p (c a s) -> p c a s", c=2, a=2)

                one_hot(Pm, posm[:, :, 0:1], e_P)
                dve.wait_ge(e_gather, NGATH * L + 1)
                dve.tensor_copy(xrow, bank[0]).then_inc(e_xrow, 1)
                one_hot(Pm, posm[:, :, 1:2], e_P)
                dve.wait_ge(e_xTp, NGATH * L + 1)
                dve.tensor_copy(xT_view(xT[0]), xT_src(4)).then_inc(e_xT, 1)
                with dve.Fori(0, NE // 2) as p:
                    for j in range(2):
                        n = p * 2 + (L * NE + j)
                        m = p * 2 + (L * NGATH + j)
                        dve.wait_ge(e_up, n + 1)
                        dve.wait_ge(e_silu, n + 2)
                        dve.tensor_tensor(actb, bank[3][:, 0:256], gsil, ALU.mult).then_inc(e_act, 1)
                        dve.wait_ge(e_gather, m + 2)
                        dve.tensor_copy(xrow, bank[0]).then_inc(e_xrow, 1)
                        one_hot(Pm, posm[:, :, bass.ds(p * 2 + (j + 2), 1)], e_P)
                        dve.wait_ge(e_aTp, n + 1)
                        dve.tensor_copy(aT_dst(aT), aT_src(5)).then_inc(e_aT, 1)
                        dve.wait_ge(e_xTp, m + 2)
                        dve.tensor_copy(xT_view(xT[1 - j]), xT_src(4)).then_inc(e_xT, 1)
                        dve.tensor_scalar(pv.unsqueeze(2), posm[:, :, bass.ds(p * 2 + j, 1)], 1.0, None,
                                          ALU.mult).then_inc(e_own, 1)
                        dve.wait_ge(e_own, n + 1)
                        more = dve.value_load(nov[0:1, bass.ds(p * 2 + j, 1)], min_val=0, max_val=5)
                        with dve.If(more > 0):
                            with dve.Fori(0, more):
                                b = dve.snap(further)
                                dve.tensor_scalar(pv, pv, -float(BLK), None, ALU.add).then_inc(v_dve, 1)
                                dve.wait_ge(v_dve, b * 7 + 1)
                                one_hot(Pov, pv, v_dve)
                                dve.wait_ge(v_pe, b * 5 + 2)
                                dve.tensor_copy(xrow_o, bank[6]).then_inc(v_dve, 1)
                                dve.wait_ge(v_pe, b * 5 + 3)
                                dve.tensor_copy(xT_view(xT_o), xT_src(7)).then_inc(v_dve, 1)
                                dve.wait_ge(v_pe, b * 5 + 4)
                                dve.wait_ge(v_act, b + 1)
                                dve.tensor_tensor(act_o, bank[7][:, 0:256], gsil_o, ALU.mult).then_inc(v_dve, 1)
                                dve.wait_ge(v_pe, b * 5 + 5)
                                dve.tensor_copy(aT_dst(aT_o), aT_src(6)).then_inc(v_dve, 1)
                                dve.wait_ge(v_pe, b * 5 + 6)
                                dve.wait_ge(v_dma, b * 32 + Y0)
                                dve.tensor_copy(y_o, bank[7]).then_inc(v_dve, 1)
                                dve.reg_add(further, further, 1)
                dve.wait_ge(gate_in, 16 * (4 * L + 4))
                for t in range(NT):
                    dve.wait_ge(yg_in[t], 32 * (L + 1))
                    y0, y1 = (modb[:, t, 0, :], modb[:, t, 1, :]) if t < 2 else (hrow[:, 0, :], hrow[:, 1, :])
                    link(dve.tensor_scalar(y0, y0, wgt[:, 0, t:t + 1], None, ALU.mult))
                    link(dve.scalar_tensor_tensor(y0, y1, wgt[:, 1, t:t + 1], y0, ALU.mult, ALU.add))
                    link(dve.tensor_tensor(y0, y0, modb[:, 2, min(t, 1), :], ALU.mult))
                    dve.tensor_tensor(xs[:, t, :], xs[:, t, :], y0, ALU.add).then_inc(x_done, 1)

        @block.tensor
        def _(pe):
            def transpose(out, in_, n=P):
                return pe.transpose(out, in_, ident[0:n, 0:n])

            def unit_in(L, name):
                s, n = landed_n(L, name)
                pe.wait_ge(landed[s], n)
                if name[0] in ("wba", "wbh"):
                    return ring[:, s, :].rearrange("p (k n) -> p k n", k=4)
                return ring[:, s, :].rearrange("p (k n) -> p k n", k=KC)

            def start_group(L, name):
                n = gno(L, name)
                if n >= 2:
                    kind, i = GROUPS[(n - 2) % NGR]
                    s, count = EVAC[kind]((n - 2) // NGR, i)
                    pe.wait_ge(s, count)
                return bank[n % 2]

            def finish_group(ins):
                ins.then_inc(group, 1)

            def mod(L, m):
                w = unit_in(L, ("mod", m))
                ps = start_group(L, ("mod", m))
                if m == 0:
                    pe.wait_ge(layer_in, 16 * (L + 1))
                for k in range(KC):
                    for j in range(4):
                        pe.matmul(ps[32 * j:32 * j + 32, 0:P], cst[:, k, :, :].rearrange("p c r -> p (c r)"),
                                  w[:, k, P * j:P * (j + 1)], start=(k == 0), stop=False)
                for j in range(4):
                    r = 4 * m + j
                    ins = pe.matmul(ps[32 * j:32 * j + 32, 0:P], ident[:, r:r + 1].broadcast_to([P, 32]), brow[:, :],
                                    start=False, stop=True)
                finish_group(ins)

            def rows(L, name, w, width, t):
                ps = start_group(L, name)
                for k in range(KC):
                    ins = pe.matmul(ps[:, 0:width], hT[:, k, t * P:(t + 1) * P], w[:, k, 0:width],
                                    start=(k == 0), stop=(k == KC - 1))
                finish_group(ins)

            def cols(L, name, w, c0, src, nk):
                ps = start_group(L, name)
                for k in range(nk):
                    ins = pe.matmul(ps[:, 0:TOK], w[:, k, c0:c0 + P], src[:, k, :], start=(k == 0), stop=(k == nk - 1))
                finish_group(ins)

            def norm(L, which):
                n = 2 * L + which
                for t in range(NT):
                    pe.wait_ge(h_ready, NT * n + t + 1)
                    for hf in range(2):
                        for c in range(4):
                            k = 4 * hf + c
                            ins = transpose(bank[2 + 2 * t + hf][:, P * c:P * (c + 1)], hrow[:, t, P * k:P * (k + 1)])
                        ins.then_inc(hT_made, 1)
                pe.wait_ge(hT_v, NT * (n + 1))
                pe.wait_ge(hT_a, NT * (n + 1))

            def att(L, k):
                if k < ATT_STEPS:
                    r, t = k // NT, k % NT
                    k0, nk = (0, P) if t == 0 else (P, 3 * P)
                    if k >= 1:
                        pe.wait_ge(at_exp, 2 * (ATT_STEPS * L + k))
                    for u in range(2):
                        ins = pe.matmul(bank[2 + u][:, 0:nk], qTa[64 * u:64 * u + 64, r, t * P:(t + 1) * P],
                                        kT[64 * u:64 * u + 64, r // 2, k0:k0 + nk], start=True, stop=True)
                    ins.then_inc(at_scores, 1)
                if 1 <= k <= ATT_STEPS:
                    nb = 1 if (k - 1) % NT == 0 else 3
                    pe.wait_ge(at_prob, ATT_STEPS * L + k)
                    if k >= 2:
                        pe.wait_ge(at_PTv, ATT_STEPS * L + k - 1)
                        pe.wait_ge(at_PTa, ATT_STEPS * L + k - 1)
                    for u in range(2):
                        for b in range(nb):
                            ins = transpose(bank[4 + u][:, P * b:P * (b + 1)], prob[:, (k - 1) % 2, u, P * b:P * (b + 1)])
                    ins.then_inc(at_PT, 1)
                if k >= 2:
                    kk = k - 2
                    r, t = kk // NT, kk % NT
                    blocks = [0] if t == 0 else [1, 2, 3]
                    pe.wait_ge(at_PTv, ATT_STEPS * L + kk + 1)
                    pe.wait_ge(at_PTa, ATT_STEPS * L + kk + 1)
                    if kk >= 1:
                        pe.wait_ge(at_outv, ATT_STEPS * L + kk)
                    g0 = HD * (r // 2)
                    for u in range(2):
                        for i, b in enumerate(blocks):
                            ins = pe.matmul(bank[6][64 * u:64 * u + 64, 0:P], Vt[:, b, g0:g0 + HD],
                                            PT[:, u, P * i:P * (i + 1)], start=(i == 0), stop=(i == len(blocks) - 1))
                    ins.then_inc(at_out, 1)

            def lev(L, s):
                pe.wait_ge(lv_W, LEV_STEPS * L + s + 1)
                for t in range(NT):
                    u = NT * s + t
                    if u >= 4:
                        pe.wait_ge(lv_mask, LEV_TILES * L + u - 3)
                    for h in range(HH):
                        c = (h * NT + t) * P
                        lhs = W[s % 2][:, c:c + P]
                        rhs = lhs if s < 2 * NLEV else qh[:, c:c + P]
                        ins = pe.matmul(bank[2 + u % 4][:, P * h:P * (h + 1)], lhs, rhs, start=True, stop=True)
                    ins.then_inc(lv_mm, 1)

            def kd(L, i):
                d, t = i // 2, ((0, 1), (0, 2))[i // 2][i % 2]
                pe.wait_ge(fin_W, 4 * L + (2 if d == 0 else 4))
                pe.wait_ge(lv_mask, LEV_TILES * (L + 1))
                for h in range(HH):
                    c = (h * NT + t) * P
                    ins = transpose(bank[2 + i][:, P * h:P * (h + 1)], E[d][:, c:c + P])
                ins.then_inc(kd_T, 1)

            def block64(dst_gate, dst_up, x, wg, wu):
                last = []
                for dst, w in ((dst_gate, wg), (dst_up, wu)):
                    if w is None:
                        continue
                    for k in range(KC):
                        for hf in range(2):
                            ins = pe.matmul(dst[64 * hf:64 * hf + 64, 0:256], x[:, k, :], w[:, k, 256 * hf:256 * (hf + 1)],
                                            start=(k == 0), stop=(k == KC - 1))
                    last.append(ins)
                return last[-1]

            def gather64(dst, sel1):
                for t in range(NT):
                    for hf in range(2):
                        ins = pe.matmul(dst[64 * hf:64 * hf + 64, :], sel1[:, t, :], hrow[:, t, 512 * hf:512 * (hf + 1)],
                                        start=(t == 0), stop=(t == NT - 1))
                return ins

            def down64(dst, x, w):
                for k in range(4):
                    for hf in range(2):
                        ins = pe.matmul(dst[64 * hf:64 * hf + 64, :], x[:, k, :], w[:, k, 512 * hf:512 * (hf + 1)],
                                        start=(k == 0), stop=(k == 3))
                return ins

            def turn(dst, src, n):
                for c in range(n):
                    ins = transpose(dst[:, P * c:P * (c + 1)], src[:, P * c:P * (c + 1)])
                return ins

            further = pe.alloc_register("pe_further")
            pe.reg_mov(further, 0)
            pe.sem_inc(v_pe, 1)
            pe.wait_ge(setup_in, 16 * 5)
            pe.wait_ge(prow_silu, 1)
            transpose(bank[2][:, 0:32], prow[:, :], 32).then_inc(prow_T, 1)
            pe.wait_ge(cst_ready, 1)

            for L in range(DEPTH):
                if L > 0:
                    pe.wait_ge(e_xrow, NGATH * L)
                    pe.wait_ge(e_y, NE * L + 1)
                for m in range(4):
                    mod(L, m)
                norm(L, 0)
                w = unit_in(L, ("q", 0))
                for t in range(NT):
                    rows(L, ("q", t), w, 512, t)
                w = unit_in(L, ("kv", 0))
                for t in range(NT):
                    rows(L, ("kv", t), w, 256, t)
                w = unit_in(L, ("hq", 0))
                for h in range(HH - 1):
                    cols(L, ("hq", h), w, P * h, hT, KC)
                for t in range(NT):
                    pe.wait_ge(qk_ready, 2 * NT * L + t + 1)
                    turn(bank[2 + t], Q[:, t, :], 4).then_inc(qk_T, 1)
                pe.wait_ge(qk_ready, 2 * NT * (L + 1))
                pe.wait_ge(ctx_in, 16 * 5 * (L + 1))
                for gk in range(NKV):
                    for b in range(4):
                        ins = transpose(bank[5 + gk][:, P * b:P * (b + 1)],
                                        Kd[:, b, gk, :, :].rearrange("p u d -> p (u d)"))
                    ins.then_inc(qk_T, 1)
                cols(L, ("hq", HH - 1), w, P * (HH - 1), hT, KC)
                pe.wait_ge(qT_ready, NT * (L + 1))
                pe.wait_ge(kT_ready, NKV * (L + 1))
                att(L, 0)
                for kind in ("ff", "fb"):
                    w = unit_in(L, (kind, 0))
                    for h in range(HH):
                        cols(L, (kind, h), w, P * h, hT, KC)
                        att(L, ATT_AT[(kind, h)])
                for kind in ("i", "g"):
                    w = unit_in(L, (kind, 0))
                    for t in range(NT):
                        rows(L, (kind, t), w, 512, t)
                        if (kind, t) in ATT_AT:
                            att(L, ATT_AT[(kind, t)])
                pe.wait_ge(at_outv, ATT_STEPS * (L + 1))
                for j in range(KC):
                    if j % 4 == 0:
                        w = unit_in(L, ("ga", j // 4))
                    cols(L, ("ga", j), w, P * (j % 4), hT, KC)
                    lev(L, LEV_AT[("ga", j)])
                for m in range(4, 12):
                    mod(L, m)
                    if ("mod", m) in LEV_AT:
                        lev(L, LEV_AT[("mod", m)])
                w = unit_in(L, ("wba", 0))
                for j in range(KC):
                    cols(L, ("wba", j), w, P * j, attnT, 4)
                    if j == 0:
                        kd(L, 0)
                        kd(L, 1)
                    if j == 1:
                        kd(L, 2)
                        kd(L, 3)
                    if j == 2:
                        pe.wait_ge(vrow_ready, NT * (L + 1))
                        for d, b, i, t in ((0, 2, 0, 0), (1, 4, 2, 0), (0, 3, 1, 1), (1, 5, 3, 2)):
                            pe.wait_ge(kd_Tv, 4 * (L + 1))
                            for h in range(HH):
                                ins = pe.matmul(bank[b][:, P * h:P * (h + 1)], kdT[d][:, i % 2, P * h:P * (h + 1)],
                                                v_rows[:, t, P * h:P * (h + 1)], start=True, stop=True)
                            ins.then_inc(st_mm, 1)
                    if j == 3:
                        for t in range(NT):
                            if t > 0:
                                pe.wait_ge(st_ready, 4 * (L + 1))
                            for h in range(HH):
                                sgm = h * NT + t
                                out = bank[O_BANK[t]][:, P * h:P * (h + 1)]
                                ins = pe.matmul(out, AT[:, sgm, :], v_rows[:, t, P * h:P * (h + 1)], start=True,
                                                stop=(t == 0))
                                if t > 0:
                                    s_f, s_b = (St, St2) if t == 1 else (St2, St)
                                    pe.matmul(out, W[1][:, sgm * P:(sgm + 1) * P], s_f[:, 0, h, :], start=False, stop=False)
                                    ins = pe.matmul(out, W[0][:, sgm * P:(sgm + 1) * P], s_b[:, 1, h, :], start=False,
                                                    stop=True)
                            ins.then_inc(o_mm, 1)
                for t in range(NT):
                    pe.wait_ge(o_ready, NT * L + t + 1)
                    turn(bank[3 + t], orow[:, t, :], 4).then_inc(o_T, 1)
                pe.wait_ge(rec_ready, NT * (L + 1))
                wh = unit_in(L, ("gh", 0))
                wb = None
                for j in range(KC):
                    if j == 4:
                        wh = unit_in(L, ("gh", 1))
                    cols(L, ("gh", j), wh, P * (j % 4), hT, KC)
                    if wb is None:
                        wb = unit_in(L, ("wbh", 0))
                    cols(L, ("wbh", j), wb, P * j, recT, HH)
                pe.wait_ge(merged, KC * (L + 1))
                for n in range(2 * NT):
                    i, t = n // NT, n % NT
                    if t == 0:
                        w = unit_in(L, ("wo", i))
                    ps = start_group(L, ("wo", n))
                    for k in range(KC):
                        ins = pe.matmul(ps, mergedT[:, k, t * P:(t + 1) * P], w[:, k, :], start=(k == 0), stop=(k == KC - 1))
                    finish_group(ins)
                norm(L, 1)
                for k in range(KC):
                    ins = pe.matmul(bank[2][0:NE, 0:TOK], wr[:, k, :], hT[:, k, :], start=(k == 0), stop=(k == KC - 1))
                ins.then_inc(rt_log, 1)
                pe.wait_ge(rt_logv, L + 1)
                for t in range(NT):
                    ins = transpose(bank[3][:, NE * t:NE * (t + 1)], rlog[0:NE, P * t:P * (t + 1)], NE)
                ins.then_inc(rt_T, 1)
                pe.wait_ge(rt_sel, L + 1)
                for t in range(NT + 1):
                    before = list(range(min(t, NT)))
                    for i, tt in enumerate(before):
                        ins = pe.matmul(bank[4][:, NE * t:NE * (t + 1)], ones, selm[:, NE * tt:NE * (tt + 1)],
                                        start=(i == 0), stop=(t == NT and i == NT - 1))
                    if t < NT:
                        ins = pe.matmul(bank[4][:, NE * t:NE * (t + 1)], tri, selm[:, NE * t:NE * (t + 1)],
                                        start=(t == 0), stop=True)
                ins.then_inc(rt_pos, 1)
                pe.wait_ge(route_ready, L + 1)
                pe.wait_ge(e_P, NPOS * L + 1)
                gather64(bank[0], Pm).then_inc(e_gather, 1)
                pe.wait_ge(e_xrow, NGATH * L + 1)
                turn(bank[4], xrow, 4).then_inc(e_xTp, 1)
                with pe.Fori(0, NE // 2) as p:
                    for j in range(2):
                        n = p * 2 + (L * NE + j)
                        m = p * 2 + (L * NGATH + j)
                        wg, wu = (ring[:, 3 * j + i, :].rearrange("p (k n) -> p k n", k=KC) for i in range(2))
                        wd = ring[:, 3 * j + 2, :].rearrange("p (k n) -> p k n", k=4)
                        pe.wait_ge(e_xT, m + 1)
                        pe.wait_ge(landed[3 * j], landed_e(L, 3 * j, p))
                        pe.wait_ge(e_silu, n + 1)
                        block64(bank[2], None, xT[j], wg, None).then_inc(e_gate, 1)
                        pe.wait_ge(landed[3 * j + 1], landed_e(L, 3 * j + 1, p))
                        pe.wait_ge(e_act, n + 1)
                        block64(None, bank[3], xT[j], None, wu).then_inc(e_up, 1)
                        pe.wait_ge(e_P, p * 2 + (L * NPOS + j + 2))
                        pe.wait_ge(e_xrow, m + 1)
                        gather64(bank[0], Pm).then_inc(e_gather, 1)
                        pe.wait_ge(e_act, n + 2)
                        turn(bank[5], actb, 2).then_inc(e_aTp, 1)
                        pe.wait_ge(e_xrow, m + 2)
                        turn(bank[4], xrow, 4).then_inc(e_xTp, 1)
                        pe.wait_ge(e_aT, n + 1)
                        pe.wait_ge(landed[3 * j + 2], landed_e(L, 3 * j + 2, p))
                        pe.wait_ge(e_y, n + 1)
                        down64(bank[1], aT, wd).then_inc(e_down, 1)
                        more = pe.value_load(nov[0:1, bass.ds(p * 2 + j, 1)], min_val=0, max_val=5)
                        with pe.If(more > 0):
                            with pe.Fori(0, more):
                                b = pe.snap(further)
                                pe.wait_ge(v_dve, b * 7 + 2)
                                gather64(bank[6], Pov).then_inc(v_pe, 1)
                                pe.wait_ge(v_dve, b * 7 + 3)
                                turn(bank[7], xrow_o, 4).then_inc(v_pe, 1)
                                pe.wait_ge(v_dve, b * 7 + 4)
                                block64(bank[6], bank[7], xT_o, wg, wu).then_inc(v_pe, 1)
                                pe.wait_ge(v_dve, b * 7 + 5)
                                turn(bank[6], act_o, 2).then_inc(v_pe, 1)
                                pe.wait_ge(v_dve, b * 7 + 6)
                                down64(bank[7], aT_o, wd).then_inc(v_pe, 1)
                                pe.reg_add(further, further, 1)


_INS = ["x_prompt", "x_sample", "cache_k", "cache_v", "state_fwd", "state_bwd", "c", "c_ctx", "norm1_w", "norm2_w",
        "w_mod", "b_mod", "w_in", "q_norm_w", "k_norm_w", "hgrn_lb_fwd", "hgrn_lb_bwd", "hgrn_norm_w", "w_br_attn",
        "w_br_hgrn", "w_out", "w_router", "b_router", "w_exp_gate", "w_exp_up", "w_exp_down"]
_OUTS = [(1, P, D), (1, 2 * P, D), (1, DEPTH, NKV, P, HD), (1, DEPTH, NKV, P, HD),
         (1, DEPTH, HH, HK, HK), (1, DEPTH, HH, HK, HK)]


def kernel(**inputs):
    import numpy as _np
    import concourse.bacc as _bacc
    from concourse import mybir as _mybir
    from concourse.bass_utils import run_bass_kernel_spmd as _run

    nc = _bacc.Bacc("TRN2", target_bir_lowering=False, num_devices=1)
    arrays, aps = {}, {}

    def given(name, a):
        arrays[f"in_{name}_dram"] = a
        aps[name] = nc.dram_tensor(f"in_{name}_dram", a.shape, _mybir.dt.from_np(a.dtype), kind="ExternalInput").ap()

    for name in _INS:
        given(name, _np.ascontiguousarray(inputs[name]))
    consts, masks = shape_constants()
    given("consts", consts)
    given("masks", masks)
    outs = [nc.dram_tensor(f"out_{i}_dram", s, F32, kind="ExternalOutput").ap() for i, s in enumerate(_OUTS)]
    build(nc, aps, outs)
    r = _run(nc, [arrays], core_ids=[0])
    return tuple(r.results[0][f"out_{i}_dram"] for i in range(len(_OUTS)))
```

```python
from contextlib import ExitStack

import numpy as np

import concourse.bass as bass
from concourse import mybir

F32 = mybir.dt.float32
I32 = mybir.dt.int32
U8 = mybir.dt.uint8
ALU = mybir.AluOpType
ACT = mybir.ActivationFunctionType
AX = mybir.AxisListType

P = 128
D = 1024
KC = D // P
NT = 3
TOK = NT * P
DEPTH = 2
NQ, NKV, HD = 8, 2, 64
HH, HK = 4, 128
SEG = HH * NT
NE, NG, EPG = 16, 4, 4
FF = 512
BLK = 64
EPS = 1e-6
GRID_W = 64
ROPE_THETA = 10000.0
MAX_EXTRA = 12
YROWS = (NE + MAX_EXTRA) * BLK
FAR = 10000.0
NGATH = NE + 1
NPOS = NE + 2

MODS = 12
MOD_FIRST = 4
MOD_BEHIND = {"hq": 4, "ff": 6, "fb": 8, "i": 10}
MOD_LEV = 12
MOD_LATE = 20
MIX_UNITS = [[("mod", m) for m in range(MOD_FIRST)]
             + [("q", 0), ("kv", 0)]
             + [u for kind, m in MOD_BEHIND.items() for u in ((kind, 0), ("mod", m), ("mod", m + 1))]
             + [("g", 0), ("ga", 0), ("ga", 1)] + [("mod", m) for m in range(MOD_LEV, MOD_LATE)]
             + [("wba", 0), ("gh", 0), ("gh", 1), ("wbh", 0), ("wo", 0), ("wo", 1)]
             + [("mod", m) for m in range(MOD_LATE, DEPTH * MODS)]]
MIX_UNITS += [[u for u in MIX_UNITS[0] if u[0] != "mod"]] * (DEPTH - 1)
MIX_SLOTS = 4
NU = [len(u) for u in MIX_UNITS]
UNIT_NO = [{u: n for n, u in enumerate(units)} for units in MIX_UNITS]
LAST_GROUP = {"q": NT - 1, "kv": NT - 1, "hq": HH - 1, "ff": HH - 1, "fb": HH - 1, "i": NT - 1, "g": NT - 1,
              "wba": KC - 1, "wbh": KC - 1}


def last_group(unit):
    kind, i = unit
    if kind == "mod":
        return unit
    if kind in ("ga", "gh"):
        return kind, 4 * i + 3
    return kind, NT * (i + 1) - 1 if kind == "wo" else LAST_GROUP[kind]


SLOT_LOADS = [[len([n for n in range(NU[L]) if n % MIX_SLOTS == s]) if s < MIX_SLOTS else 0 for s in range(6)]
              for L in range(DEPTH)]
FIRST_EXPERTS = [(4, 5, 3, 0, 1, 2)] + [(3, 0, 1, 2, 4, 5)] * (DEPTH - 1)
COL0 = {("q", 0): 0, ("kv", 0): 512, ("hq", 0): 768, ("ff", 0): 1280, ("fb", 0): 1792, ("i", 0): 2304,
        ("g", 0): 2816, ("ga", 0): 3328, ("ga", 1): 3840, ("gh", 0): 4352, ("gh", 1): 4864}



def mod_groups(first, last):
    return [(kind, m + i) for m in range(first, last, 2) for kind in ("mod", "ms") for i in range(2)]


GROUPS = [[("mod", m) for m in range(MOD_FIRST)]
          + [("q", t) for t in range(NT)] + [("kv", t) for t in range(NT)]
          + [g for kind, m in MOD_BEHIND.items()
             for g in [(kind, i) for i in range(NT if kind == "i" else HH)] + mod_groups(m, m + 2)]
          + [("g", t) for t in range(NT)] + [("ga", j) for j in range(KC)] + mod_groups(MOD_LEV, MOD_LATE)
          + [("wba", j) for j in range(KC)]
          + [(k, j) for j in range(KC) for k in ("gh", "wbh")]
          + [("wo", n) for n in range(2 * NT)] + mod_groups(MOD_LATE, DEPTH * MODS)]
GROUPS += [[g for g in GROUPS[0] if g[0] not in ("mod", "ms")]] * (DEPTH - 1)
ALL_GROUPS = [(L, g) for L in range(DEPTH) for g in GROUPS[L]]
GROUP_NO = {lg: n for n, lg in enumerate(ALL_GROUPS)}
ATT_STEPS = 4 * NT
ATT_AT = {g: k for k, g in enumerate([("hq", 3)] + [("ff", h) for h in range(HH)] + [("fb", h) for h in range(HH)]
                                     + [("i", t) for t in range(NT)] + [("g", 0), ("g", 1)])}
NLEV = 7
LEV_STEPS = 2 * NLEV + 1
LEV_AT = {g: k for k, g in enumerate([("ga", j) for j in range(KC)] + [("mod", m) for m in range(MOD_LEV, MOD_LATE - 1)])}
LEV_TILES = LEV_STEPS * NT

O_BANK = (6, 7, 2)
SMALL_LOADS = 16 * 9
Y0 = 16 * (MAX_EXTRA * BLK // P) // 3
V0 = 3

C_ID, C_TRI, C_ONE, C_IOTA, C_E64, C_OB, C_BEFORE, C_COS, C_SIN, C_SEL = 0, 128, 256, 384, 448, 464, 480, 496, 624, 752
NCONST = 784


def shape_constants():
    c = np.zeros((P, NCONST), np.float32)
    c[:, C_ID:C_ID + P] = np.eye(P)
    c[:, C_TRI:C_TRI + P] = np.triu(np.ones((P, P)), 1)
    c[:, C_ONE:C_ONE + P] = 1.0
    c[:, C_IOTA:C_IOTA + BLK] = np.arange(BLK)
    c[:, C_E64:C_E64 + NE] = BLK * np.arange(NE)
    c[:, C_OB:C_OB + NE] = (NE - 1) * BLK - BLK * np.arange(NE)
    c[:, C_BEFORE:C_BEFORE + 16] = np.tril(np.ones((4, 4)), -1).reshape(-1)
    for cnd in range(2):
        c[16 * cnd::32, C_SEL + 16 * cnd:C_SEL + 16 * (cnd + 1)] = 1.0
    tok = np.arange(2 * P)
    inv = np.float32(ROPE_THETA) ** (-np.arange(0, 32, 2, dtype=np.float32) / np.float32(32))
    ar = (tok // GRID_W).astype(np.float32)[:, None] * inv
    ac = (tok % GRID_W).astype(np.float32)[:, None] * inv
    ang = np.concatenate([ar, ar, ac, ac], 1)
    sign = np.tile(np.repeat([-1.0, 1.0], 16), 2).astype(np.float32)
    for t in range(2):
        c[:, C_COS + HD * t:C_COS + HD * (t + 1)] = np.cos(ang[t * P:(t + 1) * P])
        c[:, C_SIN + HD * t:C_SIN + HD * (t + 1)] = np.sin(ang[t * P:(t + 1) * P]) * sign
    masks = np.zeros((P, LEV_STEPS, P), np.int32)
    s, t = np.arange(P)[:, None], np.arange(P)[None, :]
    for lev in range(NLEV):
        m = 64 >> lev
        same = (s // (2 * m)) == (t // (2 * m))
        masks[:, 2 * lev] = same & (s % (2 * m) < m) & (t % (2 * m) >= m)
        masks[:, 2 * lev + 1] = same & (s % (2 * m) >= m) & (t % (2 * m) < m)
    masks[:, 2 * NLEV] = s == t
    return c, masks.reshape(P, -1)


def build(nc, a, o):
    y_prompt, y_sample, new_k, new_v, new_sf, new_sb = o
    mod_scr = nc.dram_tensor("mod_scr", [DEPTH, 2, 6 * D], F32, kind="Internal").ap()
    y_scr = nc.dram_tensor("y_scr", [YROWS, D], F32, kind="Internal").ap()

    with ExitStack() as ctx:
        def sb(name, shape, dt=F32):
            return ctx.enter_context(nc.sbuf_tensor(name, shape, dt))

        def sem(name):
            return ctx.enter_context(nc.semaphore(name))

        ring = sb("ring", [P, 6, 4096])
        xs = sb("xs", [P, NT, D])
        hrow = sb("hrow", [P, NT, D])
        hT = sb("hT", [P, KC, TOK])
        modb = sb("modb", [P, 3, 2, D])
        nw = sb("nw", [P, D])
        gen = sb("gen", [P, 9240])
        const = sb("const", [P, NCONST])
        masks = sb("masks", [P, LEV_STEPS, P], U8)
        prow = sb("prow", [32, P])
        lbT = sb("lbT", [P, DEPTH, 2, HH])
        omT = sb("omT", [P, DEPTH, 2, HH])
        lbe = sb("lbe", [P, 4, 8])
        qnw = sb("qnw", [P, DEPTH, HD])
        knw = sb("knw", [P, DEPTH, HD])
        hnw = sb("hnw", [P, DEPTH, HK])
        cst = sb("cst", [P, KC, 2, 16])
        brow = sb("brow", [P, DEPTH, P])
        wr = sb("wr", [P, KC, NE])
        br = sb("br", [P, NE])
        stat = sb("stat", [P, 96])
        dec = sb("dec", [P, 2, SEG])
        lraw = sb("lraw", [P, 16])
        half = sb("half", [P, 16])
        idx = sb("idx", [P, 2, NT], I32)
        wgt = sb("wgt", [P, 2, NT])
        nov = sb("nov", [1, NE], I32)

        ident = const[:, C_ID:C_ID + P]
        tri = const[:, C_TRI:C_TRI + P]
        ones = const[:, C_ONE:C_ONE + P]
        iota = const[:, C_IOTA:C_IOTA + BLK]

        S = ring[:, 4:6, :].rearrange("p a b -> p (a b)")
        Q = S[:, 0:1536].rearrange("p (t c) -> p t c", t=NT)
        sg = Q
        Kd = S[:, 1536:2560].rearrange("p (b g u d) -> p b g u d", b=4, g=NKV, u=2)
        Vt = S[:, 2560:3072].rearrange("p (b c) -> p b c", b=4)
        qTa = S[:, 3072:4608].rearrange("p (r t) -> p r t", r=4)
        kT = S[:, 4608:5632].rearrange("p (g k) -> p g k", g=NKV)
        prob = S[:, 5632:7168].rearrange("p (b u k) -> p b u k", b=2, u=2)
        PT = S[:, 7168:7936].rearrange("p (u k) -> p u k", u=2)
        AT = S[:, 1536:3072].rearrange("p (s t) -> p s t", s=SEG)
        E = [S[:, 3072:4608], S[:, 4608:6144]]
        orow = E[1].rearrange("p (t c) -> p t c", t=NT)
        MB = modb[:, 0:2].rearrange("p a b c -> p (a b c)")
        attnT = MB[:, 0:1536].rearrange("p (r t) -> p r t", r=4)
        W = [S[:, 6144:7680], MB[:, 1536:3072]]
        St = MB[:, 3072:4096].rearrange("p (d h v) -> p d h v", d=2, h=HH)
        scratch = W[1]
        qh = gen[:, 0:1536]
        kg = [gen[:, 1536:3072], gen[:, 3072:4608]]
        Cflat = [gen[:, 4608:6156], gen[:, 6156:7704]]
        Cs = [c.rearrange("p (s t) -> p s t", s=SEG) for c in Cflat]
        v_rows = gen[:, 7704:9240].rearrange("p (t c) -> p t c", t=NT)
        recT = qh.rearrange("p (h t) -> p h t", h=HH)
        kdT = [c[:, 0:1024].rearrange("p (b c) -> p b c", b=2) for c in Cflat]
        St_out = kg[0][:, 0:1024].rearrange("p (d h v) -> p d h v", d=2, h=HH)
        St2 = kg[1][:, 0:1024].rearrange("p (d h v) -> p d h v", d=2, h=HH)
        mergedT = hrow[:, :, :].rearrange("p t c -> p (t c)").rearrange("p (j t) -> p j t", j=KC)
        gs = E[0][:, 0:768].rearrange("p (b t) -> p b t", b=2)
        wo_tmp = W[0][:, 0:1024].rearrange("p (b c) -> p b c", b=2)

        off = [0]

        def g(n):
            off[0] += n
            assert off[0] <= 9240 - 512 * (DEPTH * MODS - MOD_LATE)
            return gen[:, off[0] - n:off[0]]

        Pm = g(NT * BLK).rearrange("p (t s) -> p t s", t=NT)
        xrow = g(512)
        xT = [g(512).rearrange("p (k s) -> p k s", k=KC) for _ in range(2)]
        gsil, actb = g(256), g(256)
        aT = g(256).rearrange("p (k s) -> p k s", k=4)
        ysb = [g(512) for _ in range(2)]
        Pov = g(NT * BLK).rearrange("p (t s) -> p t s", t=NT)
        xrow_o = g(512)
        xT_o = g(512).rearrange("p (k s) -> p k s", k=KC)
        gsil_o, act_o = g(256), g(256)
        aT_o = g(256).rearrange("p (k s) -> p k s", k=4)
        y_o = g(512)
        pv = g(NT)
        posm = g(NT * NPOS).rearrange("p (t e) -> p t e", t=NT)
        rlog = y_o[:, 0:TOK]
        sc, sel, rank, top, oh0, oh1, selm, pos, t48, idxa = [g(NT * NE) for _ in range(10)]
        cmp1, cmp2 = g(192), g(192)
        gsum, grank, gb = g(12), g(12), g(12)
        cnt, novf, ovs, ob = g(16), g(16), g(16), g(16)
        idxf, wsum, wrec = g(6), g(NT), g(NT)
        results = gen[:, 0:2 * NT * D].rearrange("p (t c d) -> p t c d", t=NT, c=2)
        zeros = S[:, 7936:8192]
        masks32 = S[:, 0:LEV_STEPS * P].bitcast(I32)

        pG = [ctx.enter_context(nc.psum_tensor(f"pG{i}", [P, 512], F32)) for i in range(2)]
        pS = ctx.enter_context(nc.psum_tensor("pS", [P, 2, 512], F32))
        pX = [ctx.enter_context(nc.psum_tensor(f"pX{i}", [P, 512], F32)) for i in range(4)]
        bank = [pG[0][:, :], pG[1][:, :], pS[:, 0, :], pS[:, 1, :]] + [x[:, :] for x in pX]

        landed = [sem(f"landed{s}") for s in range(6)]
        setup_in = sem("setup_in")
        prow_silu = sem("prow_silu")
        prow_T = sem("prow_T")
        cst_ready = sem("cst_ready")
        masks_ready = sem("masks_ready")
        lb_ready = sem("lb_ready")
        small_in = sem("small_in")
        x_in = sem("x_in")
        zeroed = sem("zeroed")
        layer_in = sem("layer_in")
        nw_in = sem("nw_in")
        ctx_in = sem("ctx_in")
        mod_stored = [sem("mod_stored0"), sem("mod_stored1")]
        mod_evac = sem("mod_evac")
        ms_evac = sem("ms_evac")
        mod_bc = sem("mod_bc")
        mod_bcv = sem("mod_bcv")
        mods_in = sem("mods_in")
        gate_in = sem("gate_in")
        sq_done = sem("sq_done")
        ms_done = sem("ms_done")
        rstd_done = sem("rstd_done")
        h_ready = sem("h_ready")
        hT_made = sem("hT_made")
        hT_v = sem("hT_v")
        hT_a = sem("hT_a")
        group = sem("group")
        qkv_evac = sem("qkv_evac")
        f_sig = sem("f_sig")
        wba_done = sem("wba_done")
        wbh_done = sem("wbh_done")
        wo_evac = sem("wo_evac")
        qk_ms = sem("qk_ms")
        qk_ready = sem("qk_ready")
        qk_T = sem("qk_T")
        qT_ready = sem("qT_ready")
        kT_ready = sem("kT_ready")
        at_scores = sem("at_scores")
        at_max = sem("at_max")
        at_exp = sem("at_exp")
        at_prob = sem("at_prob")
        at_PT = sem("at_PT")
        at_PTv = sem("at_PTv")
        at_PTa = sem("at_PTa")
        at_out = sem("at_out")
        at_outv = sem("at_outv")
        sig_done = sem("sig_done")
        hgq_ready = sem("hgq_ready")
        f_done = sem("f_done")
        ln_done = sem("ln_done")
        C_ready = sem("C_ready")
        vrow_ready = sem("vrow_ready")
        sg_mul = sem("sg_mul")
        sg_ready = sem("sg_ready")
        lv_D = sem("lv_D")
        lv_E = sem("lv_E")
        lv_W = sem("lv_W")
        lv_mm = sem("lv_mm")
        lv_mask = sem("lv_mask")
        fin_D = sem("fin_D")
        fin_E = sem("fin_E")
        fin_W = sem("fin_W")
        kd_T = sem("kd_T")
        kd_Tv = sem("kd_Tv")
        st_mm = sem("st_mm")
        st_ready = sem("st_ready")
        st_stored = sem("st_stored")
        kv_stored = sem("kv_stored")
        o_mm = sem("o_mm")
        o_sq = sem("o_sq")
        o_ms = sem("o_ms")
        o_rstd = sem("o_rstd")
        o_ready = sem("o_ready")
        o_T = sem("o_T")
        rec_ready = sem("rec_ready")
        ga_ready = sem("ga_ready")
        gh_ready = sem("gh_ready")
        merged = sem("merged")
        x_mid = sem("x_mid")
        rt_log = sem("rt_log")
        rt_logv = sem("rt_logv")
        rt_T = sem("rt_T")
        rt_sc = sem("rt_sc")
        rt_sel = sem("rt_sel")
        rt_pos = sem("rt_pos")
        route_ready = sem("route_ready")
        e_P = sem("e_P")
        e_gather = sem("e_gather")
        e_xrow = sem("e_xrow")
        e_xTp = sem("e_xTp")
        e_xT = sem("e_xT")
        e_gate = sem("e_gate")
        e_up = sem("e_up")
        e_silu = sem("e_silu")
        e_act = sem("e_act")
        e_aTp = sem("e_aTp")
        e_aT = sem("e_aT")
        e_down = sem("e_down")
        e_y = sem("e_y")
        e_ydma = [sem("e_ydma0"), sem("e_ydma1")]
        v_pe = sem("v_pe")
        v_dve = sem("v_dve")
        v_act = sem("v_act")
        v_dma = sem("v_dma")
        y_all = sem("y_all")
        yg_in = [sem(f"yg_in{t}") for t in range(NT)]
        x_done = sem("x_done")
        dve_own = sem("dve_own")
        pool_own = sem("pool_own")
        e_own = sem("e_own")
        out_done = sem("out_done")

        block = ctx.enter_context(nc.Block())

        def loads_before(L, s):
            return sum(SLOT_LOADS[l][s] + NE // 2 for l in range(L))

        def landed_n(L, name):
            n = UNIT_NO[L][name]
            s = n % MIX_SLOTS
            return s, 16 * (loads_before(L, s) + n // MIX_SLOTS + 1)

        def landed_e(L, s, p):
            return 16 * (loads_before(L, s) + SLOT_LOADS[L][s]) + (p + 1) * 16

        def gno(L, name):
            return GROUP_NO[L, name]

        EVAC = {
            "mod": lambda L, i: (mod_evac, i + 1),
            "ms": lambda L, i: (ms_evac, i - MOD_FIRST + 1),
            "q": lambda L, i: (qkv_evac, 2 * NT * L + i + 1),
            "kv": lambda L, i: (qkv_evac, 2 * NT * L + NT + i + 1),
            "hq": lambda L, i: (hgq_ready, HH * L + i + 1),
            "ff": lambda L, i: (f_sig, 2 * HH * L + i + 1),
            "fb": lambda L, i: (f_sig, 2 * HH * L + HH + i + 1),
            "i": lambda L, i: (vrow_ready, NT * L + i + 1),
            "g": lambda L, i: (sg_mul, NT * L + i + 1),
            "ga": lambda L, i: (ga_ready, KC * L + i + 1),
            "wba": lambda L, i: (wba_done, KC * L + i + 1),
            "gh": lambda L, i: (gh_ready, KC * L + i + 1),
            "wbh": lambda L, i: (wbh_done, KC * L + i + 1),
            "wo": lambda L, i: (wo_evac, 2 * NT * L + i + 1),
        }

        def mod_parts(m):
            if m < MOD_LATE:
                return modb[:, 2, 0, 512 * (m % 2):512 * (m % 2 + 1)]
            c0 = 9240 - 512 * (DEPTH * MODS - m)
            return gen[:, c0:c0 + 512]

        def mods_stored(m):
            return 32 * (m - MOD_FIRST) // 2

        def bc(ap, shape, axis):
            return ap.unsqueeze(axis).broadcast_to(shape)

        @block.sync
        def _(sp):
            sp.dma_start(prow[0:8, :], a["c_ctx"].rearrange("(k c) -> k c", k=8)).then_inc(setup_in, 16)
            sp.dma_start(prow[8:16, :], a["c"].rearrange("b (k c) -> (b k) c", k=8)).then_inc(setup_in, 16)
            for d, n in enumerate(("hgrn_lb_fwd", "hgrn_lb_bwd")):
                sp.dma_start(prow[16 + 8 * d:24 + 8 * d, :],
                             a[n].rearrange("l (h c) -> (l h) c", h=HH)).then_inc(setup_in, 16)
            sp.dma_start(const[:, :], a["consts"]).then_inc(setup_in, 16)
            ov = sp.alloc_register("sp_further")
            sp.reg_mov(ov, 0)

            def unit(L, name):
                s = UNIT_NO[L][name] % MIX_SLOTS
                kind, i = name
                dst = ring[:, s, :].rearrange("p (k n) -> p k n", k=KC)
                if kind == "mod":
                    c0 = 512 * (i % MODS)
                    src = a["w_mod"][i // MODS].rearrange("(k p) n -> p k n", p=P)[:, :, c0:c0 + 512]
                elif kind == "wba" or kind == "wbh":
                    dst = ring[:, s, :].rearrange("p (k n) -> p k n", k=4)
                    src = a["w_br_attn" if kind == "wba" else "w_br_hgrn"][L].rearrange("(k p) n -> p k n", p=P)
                elif kind == "wo":
                    src = a["w_out"][L].rearrange("(k p) n -> p k n", p=P)[:, :, 512 * i:512 * (i + 1)]
                else:
                    width = 256 if kind == "kv" else 512
                    c0 = COL0[name]
                    dst = dst[:, :, 0:width]
                    src = a["w_in"][L].rearrange("(k p) n -> p k n", p=P)[:, :, c0:c0 + width]
                sp.dma_start(dst, src).then_inc(landed[s], 16)

            def expert(L, e, s0, part):
                if part < 2:
                    src = a[("w_exp_gate", "w_exp_up")[part]][L, e, :, :].rearrange("(k p) n -> p k n", p=P)
                    dst = ring[:, s0 + part, :].rearrange("p (k n) -> p k n", k=KC)
                else:
                    src = a["w_exp_down"][L, e, :, :].rearrange("(k p) n -> p k n", p=P)
                    dst = ring[:, s0 + part, :].rearrange("p (k n) -> p k n", k=4)
                return sp.dma_start(dst, src).then_inc(landed[s0 + part], 16)

            def further_done(e, gate_and_up=False):
                sp.reg_add(ov, ov, sp.value_load(nov[0:1, bass.ds(e, 1)], min_val=0, max_val=5))
                sp.wait_ge(v_pe, sp.snap(ov) * 5 + (V0 - 2 if gate_and_up else V0))

            for L in range(DEPTH):
                for n, name in enumerate(MIX_UNITS[L]):
                    if n >= MIX_SLOTS:
                        sp.wait_ge(group, gno(L, last_group(MIX_UNITS[L][n - MIX_SLOTS])) + 1)
                    elif L > 0:
                        if n == 0:
                            sp.wait_ge(e_down, L * NE - 1)
                            further_done(NE - 2)
                        if n == 2:
                            sp.wait_ge(yg_in[NT - 1], 32 * L)
                        if n == 3:
                            sp.wait_ge(e_down, L * NE)
                            further_done(NE - 1)
                    unit(L, name)
                for slot in FIRST_EXPERTS[L]:
                    if slot < MIX_SLOTS:
                        last = max(n for n in range(NU[L]) if n % MIX_SLOTS == slot)
                        sp.wait_ge(group, gno(L, last_group(MIX_UNITS[L][last])) + 1)
                    elif slot == MIX_SLOTS:
                        sp.wait_ge(x_mid, 2 * NT * (L + 1))
                        if L == 0:
                            for s in (*e_ydma, v_dma):
                                sp.wait_ge(s, Y0)
                    expert(L, slot // 3, 3 * (slot // 3), slot % 3)
                sp.wait_ge(route_ready, L + 1)
                with sp.Fori(1, NE // 2) as p:
                    for j in range(2):
                        sp.wait_ge(e_gate, p * 2 + (L * NE + j - 1))
                        further_done(p * 2 + (j - 2), gate_and_up=True)
                        expert(L, p * 2 + j, 3 * j, 0)
                        sp.wait_ge(e_up, p * 2 + (L * NE + j - 1))
                        expert(L, p * 2 + j, 3 * j, 1)
                        sp.wait_ge(e_down, p * 2 + (L * NE + j - 1))
                        sp.wait_ge(v_pe, sp.snap(ov) * 5 + V0)
                        expert(L, p * 2 + j, 3 * j, 2)
            sp.wait_ge(x_done, NT * (DEPTH - 1) + 1)
            sp.dma_start(y_prompt[0], xs[:, 0, :]).then_inc(out_done, 16)
            for t in range(1, NT):
                sp.wait_ge(x_done, NT * (DEPTH - 1) + t + 1)
                sp.dma_start(y_sample[0, (t - 1) * P:t * P, :], xs[:, t, :]).then_inc(out_done, 16)
            sp.wait_ge(out_done, 16 * NT)
            sp.wait_ge(st_stored, 16 * 2 * DEPTH)
            sp.wait_ge(kv_stored, 16 * 2 * DEPTH)

        @block.gpsimd
        def _(pool):
            own = [0]

            def link(ins):
                own[0] += 1
                ins.then_inc(pool_own, 1)
                pool.wait_ge(pool_own, own[0])

            def load_norm(L, which):
                src = a[("norm1_w", "norm2_w")[which]][L:L + 1, :]
                pool.dma_start(nw[:, :], src.broadcast_to([P, D])).then_inc(nw_in, 16)

            def load_mod(L, v, dst, s):
                for cnd in range(2):
                    src = mod_scr[L, cnd:cnd + 1, v * D:(v + 1) * D]
                    pool.dma_start(modb[:, dst, cnd, :], src.broadcast_to([P, D])).then_inc(s, 16)

            def mean_root(s, n, stat0, width, done):
                pool.wait_ge(s, n)
                return pool.tensor_tensor(stat[:, stat0:stat0 + width], stat[:, stat0:stat0 + width],
                                          half[:, 0:width], ALU.pow).then_inc(done, 1)

            pool.wait_ge(zeroed, 1)
            for L in range(DEPTH):
                pool.dma_start(brow[0:6 * D // P, L, :], a["b_mod"][L].rearrange("(r c) -> r c", c=P)).then_inc(layer_in, 16)
            load_norm(0, 0)
            pool.wait_ge(landed[1], 16)
            pool.dma_start(xs[:, 0, :], a["x_prompt"][0]).then_inc(x_in, 16)
            pool.dma_start(xs[:, 1:3, :], a["x_sample"][0].rearrange("(t p) c -> p t c", p=P)).then_inc(x_in, 16)
            for n, (dst, name, w) in enumerate(((qnw, "q_norm_w", HD), (knw, "k_norm_w", HD), (hnw, "hgrn_norm_w", HK))):
                for L in range(DEPTH):
                    pool.dma_start(dst[:, L, :], a[name][L:L + 1, :].broadcast_to([P, w])).then_inc(small_in, 16)
            pool.dma_start(wr[:, :, :], a["w_router"].rearrange("(k p) e -> p k e", p=P)).then_inc(small_in, 16)
            pool.dma_start(br[:, :], a["b_router"].rearrange("(a e) -> a e", a=1).broadcast_to([P, NE])).then_inc(small_in, 16)
            pool.dma_start(masks32, a["masks"]).then_inc(small_in, 16)
            for L in range(DEPTH):
                mean_root(ms_done, 2 * L + 1, 0, NT, rstd_done)
                pool.wait_ge(h_ready, 2 * NT * L + NT)
                ck = a["cache_k"][0, L].rearrange("g k d -> k g d")
                for u in range(2):
                    pool.dma_start(Kd[:, 3, :, u, :], ck).then_inc(ctx_in, 16)
                pool.dma_start(Vt[:, 3, :].rearrange("p (g d) -> p g d", g=NKV),
                               a["cache_v"][0, L].rearrange("g k d -> k g d")).then_inc(ctx_in, 16)
                for d, n in enumerate(("state_fwd", "state_bwd")):
                    pool.dma_start(St[:, d, :, :], a[n][0, L].rearrange("h k v -> k h v")).then_inc(ctx_in, 16)
                load_norm(L, 1)
                for n in range(2 * NT):
                    isq, t = n < NT, n % NT
                    heads = NQ if isq else NKV
                    r0 = 16 + 8 * n
                    mean_root(qk_ms, 2 * NT * L + n + 1, r0, heads, pool_own)
                    own[0] += 1
                    pool.wait_ge(pool_own, own[0])
                    x = Q[:, t, :].rearrange("p (h d) -> p h d", h=NQ) if isq else Kd[:, t, :, 0, :]
                    w = (qnw if isq else knw)[:, L, :]
                    link(pool.tensor_tensor(x, x, bc(stat[:, r0:r0 + heads], [P, heads, HD], 2), ALU.mult))
                    last = pool.tensor_tensor(x, x, bc(w, [P, heads, HD], 1), ALU.mult)
                    if t > 0:
                        link(last)
                        cos = const[:, C_COS + HD * (t - 1):C_COS + HD * t]
                        sin = const[:, C_SIN + HD * (t - 1):C_SIN + HD * t].rearrange("p (a b c) -> p a b c", a=2, b=2)
                        A = scratch[:, 0:HD * heads].rearrange("p (h d) -> p h d", h=heads)
                        B = scratch[:, 512:512 + HD * heads].rearrange("p (h d) -> p h d", h=heads)
                        x5 = x.rearrange("p h (a b c) -> p h a b c", a=2, b=2)
                        B5 = B.rearrange("p h (a b c) -> p h a b c", a=2, b=2)
                        pool.tensor_tensor(A, x, bc(cos, [P, heads, HD], 1), ALU.mult)
                        for b in range(2):
                            last = pool.tensor_tensor(B5[:, :, :, b, :], x5[:, :, :, 1 - b, :],
                                                      bc(sin[:, :, b, :], [P, heads, 2, 16], 1), ALU.mult)
                        link(last)
                        last = pool.tensor_tensor(x, A, B, ALU.add)
                    if not isq:
                        link(last)
                        last = pool.tensor_scalar(Kd[:, t, :, 1, :], x, 1.0, None, ALU.mult)
                    last.then_inc(qk_ready, 1)
                for t in range(NT):
                    pool.wait_ge(sg_mul, NT * L + t + 1)
                    s4 = sg[:, t, :].rearrange("p (h v) -> p h v", h=HH)
                    pool.tensor_tensor(s4, s4, bc(hnw[:, L, :], [P, HH, HK], 1), ALU.mult).then_inc(sg_ready, 1)
                pool.wait_ge(at_outv, ATT_STEPS * (L + 1))
                for s in range(2 * NLEV):
                    m, d = 64 >> (s // 2), s % 2
                    pool.wait_ge(C_ready, 2 * L + d + 1)
                    if s >= 2:
                        pool.wait_ge(lv_W, LEV_STEPS * L + s - 1)
                    base = Cs[d][:, :, 1 - d:129 - d].rearrange("p s (b u m) -> p s b u m", u=2, m=m)
                    mid = Cs[d][:, :, m:m + 128 - 2 * m + 1:2 * m] if m < 64 else Cs[d][:, :, 64:65]
                    mid = mid.unsqueeze(3).broadcast_to([P, SEG, 64 // m, m])
                    out = E[d].rearrange("p (s b u m) -> p s b u m", s=SEG, u=2, m=m)
                    pool.tensor_tensor(out[:, :, :, 0, :], mid, base[:, :, :, 0, :], ALU.subtract)
                    pool.tensor_tensor(out[:, :, :, 1, :], base[:, :, :, 1, :], mid, ALU.subtract).then_inc(lv_D, 1)
                pool.wait_ge(lv_W, LEV_STEPS * (L + 1))
                for d, dst in ((0, E[0]), (1, W[0])):
                    if d == 1:
                        pool.wait_ge(lv_mm, LEV_TILES * (L + 1))
                    end = Cs[d][:, :, 128:129].broadcast_to([P, SEG, P])
                    pool.tensor_tensor(dst.rearrange("p (s t) -> p s t", s=SEG), end, Cs[d][:, :, 1 - d:129 - d],
                                       ALU.subtract).then_inc(fin_D, 1)
                for t in range(NT):
                    mean_root(o_ms, NT * L + t + 1, 64 + 4 * t, HH, o_rstd)
                for b in range(2):
                    pool.wait_ge(mod_stored[b], mods_stored(MOD_LATE if L == 0 else DEPTH * MODS))
                load_mod(L, 2, 2, gate_in)
                pool.wait_ge(group, gno(L, ("wba", KC - 1)) + 1)
                pool.wait_ge(o_mm, NT * (L + 1))
                pool.wait_ge(st_ready, 4 * (L + 1))
                load_mod(L, 3, 0, mods_in)
                load_mod(L, 4, 1, mods_in)
                mean_root(ms_done, 2 * L + 2, 0, NT, rstd_done)
                pool.wait_ge(x_mid, 2 * NT * (L + 1))
                load_mod(L, 5, 2, gate_in)
                if L + 1 < DEPTH:
                    pool.wait_ge(h_ready, 2 * NT * (L + 1))
                    load_norm(L + 1, 0)
                    load_mod(L + 1, 0, 0, mods_in)
                    load_mod(L + 1, 1, 1, mods_in)
                pool.wait_ge(y_all, L + 1)
                pool.wait_ge(e_own, NE * (L + 1))
                for t in range(NT):
                    for c in range(2):
                        pool.indirect_dma_start(results[:, t, c, :], None, y_scr[:, :],
                                                bass.IndirectOffsetOnAxis(ap=idx[:, c, t:t + 1], axis=0)
                                                ).then_inc(yg_in[t], 16)

        @block.scalar
        def _(act):
            def sync_group(L, name):
                act.wait_ge(group, gno(L, name) + 1)
                return bank[gno(L, name) % 2]

            act.sem_inc(e_silu, 1)
            act.sem_inc(e_y, 1)
            act.wait_ge(zeroed, 1)
            for i, r in enumerate(range(NE * BLK, YROWS, P)):
                act.dma_start(y_scr[r:r + P, :].rearrange("p (a c) -> p a c", a=4),
                              bc(zeros, [P, 4, 256], 1)).then_inc((*e_ydma, v_dma)[i % 3], 16)
            act.wait_ge(setup_in, 16 * 5)
            act.activation(prow[0:16, :], prow[0:16, :], ACT.Silu).then_inc(prow_silu, 1)
            act.wait_ge(lb_ready, 1)
            act.activation(lbe[:, 1:3, :], lbe[:, 1:3, :], ACT.Exp).then_inc(lb_ready, 1)
            further = act.alloc_register("act_further")
            further_l = act.alloc_register("act_further_layer")
            act.reg_mov(further, 0)

            def mod_copy(m):
                ps = sync_group(0, ("mod", m))
                if 2 <= m < MOD_FIRST + 2:
                    act.wait_ge(mod_bc, min(m - 1, MOD_FIRST))
                elif MOD_FIRST + 2 <= m < MOD_LATE:
                    act.wait_ge(mod_stored[m % 2], mods_stored(m - m % 2))
                act.copy(mod_parts(m), ps).then_inc(mod_evac, 1)

            def mod_store(m):
                ps = sync_group(0, ("ms", m))
                act.copy(mod_parts(m)[0:32, :], ps[0:32, :]).then_inc(ms_evac, 1)
                act.wait_ge(ms_evac, m - MOD_FIRST + 1)
                for cnd in range(2):
                    dst = mod_scr[m // MODS, cnd:cnd + 1, 512 * (m % MODS):512 * (m % MODS + 1)]
                    act.dma_start(dst, mod_parts(m)[16 * cnd:16 * cnd + 1, :]).then_inc(mod_stored[m % 2], 16)

            def mods_behind(L, kind):
                if L == 0:
                    m = MOD_BEHIND[kind]
                    mod_copy(m)
                    mod_copy(m + 1)
                    mod_store(m)
                    mod_store(m + 1)

            def norm(L, which):
                for t in range(NT):
                    squares = hrow[:, t, :]
                    if which == 0:
                        squares = gen[:, D * (2 * NT + t):D * (2 * NT + t + 1)]
                        if L == 0:
                            act.wait_ge(x_in, 32)
                        else:
                            act.wait_ge(x_done, NT * (L - 1) + t + 1)
                    elif t == 0:
                        act.wait_ge(x_mid, 2 * NT * (L + 1))
                    act.activation(squares, xs[:, t, :], ACT.Square,
                                   accum_out=stat[:, t:t + 1]).then_inc(sq_done, 1)
                if L == 0 and which == 1:
                    mod_copy(MOD_LATE)
                    mod_copy(MOD_LATE + 1)
                for t in range(NT):
                    act.wait_ge(hT_made, 2 * NT * (2 * L + which) + 2 * t + 2)
                    act.copy(hT[:, 4:8, t * P:(t + 1) * P],
                             bank[3 + 2 * t].rearrange("p (k t) -> p k t", k=4)).then_inc(hT_a, 1)

            def att(L, k):
                if k < ATT_STEPS:
                    nk = P if k % NT == 0 else 3 * P
                    c0 = 80 + 8 * (k % 2)
                    act.wait_ge(at_max, ATT_STEPS * L + k + 1)
                    if k >= 2:
                        act.wait_ge(at_PT, ATT_STEPS * L + k - 1)
                    for u in range(2):
                        act.activation(prob[:, k % 2, u, 0:nk], bank[2 + u][:, 0:nk], ACT.Exp,
                                       bias=stat[:, c0 + 2 + u:c0 + 3 + u], scale=float(HD) ** -0.5,
                                       accum_out=stat[:, c0 + 4 + u:c0 + 5 + u]).then_inc(at_exp, 1)
                if 1 <= k <= ATT_STEPS:
                    nk = P if (k - 1) % NT == 0 else 3 * P
                    act.wait_ge(at_PT, ATT_STEPS * L + k)
                    if k >= 2:
                        act.wait_ge(at_out, ATT_STEPS * L + k - 1)
                    act.copy(PT[:, 1, 0:nk], bank[5][:, 0:nk]).then_inc(at_PTa, 1)

            def lev(L, s):
                if s < 2 * NLEV:
                    act.wait_ge(lv_D, 2 * NLEV * L + s + 1)
                    act.activation(E[s % 2], E[s % 2], ACT.Exp).then_inc(lv_E, 1)

            for L in range(DEPTH):
                if L == 0:
                    for m in range(MOD_FIRST):
                        mod_copy(m)
                norm(L, 0)
                for h in range(HH - 1):
                    sync_group(L, ("hq", h))
                    act.activation(qh[:, h * TOK:(h + 1) * TOK], bank[gno(L, ("hq", h)) % 2][:, 0:TOK],
                                   ACT.Sigmoid).then_inc(sig_done, 1)
                act.wait_ge(qk_T, 5 * (L + 1))
                for gk in range(NKV):
                    act.copy(kT[:, gk, :], bank[5 + gk]).then_inc(kT_ready, 1)
                act.wait_ge(qk_ready, 2 * NT * L + NT + 1)
                act.dma_start(new_k[0, L].rearrange("g k d -> k g d"), Kd[:, 0, :, 0, :]).then_inc(kv_stored, 16)
                act.wait_ge(qkv_evac, 2 * NT * L + NT + 1)
                act.dma_start(new_v[0, L].rearrange("g k d -> k g d"),
                              Vt[:, 0, :].rearrange("p (g d) -> p g d", g=NKV)).then_inc(kv_stored, 16)
                ps = sync_group(L, ("hq", HH - 1))
                act.activation(qh[:, (HH - 1) * TOK:HH * TOK], ps[:, 0:TOK], ACT.Sigmoid).then_inc(sig_done, 1)
                att(L, 0)
                mods_behind(L, "hq")
                if L > 0:
                    act.wait_ge(st_stored, 16 * 2 * L)
                for d, kind in enumerate(("ff", "fb")):
                    for h in range(HH):
                        ps = sync_group(L, (kind, h))
                        act.activation(kg[d][:, h * TOK:(h + 1) * TOK], ps[:, 0:TOK],
                                       ACT.Sigmoid).then_inc(f_sig, 1)
                        att(L, ATT_AT[(kind, h)])
                    mods_behind(L, kind)
                    act.wait_ge(f_done, 2 * HH * L + HH * (d + 1))
                    if d == 0:
                        act.wait_ge(qk_ready, 2 * NT * (L + 1))
                    else:
                        act.wait_ge(C_ready, 2 * L + 1)
                    act.activation(scratch, kg[d], ACT.Ln).then_inc(ln_done, 1)
                for t in range(NT):
                    ps = sync_group(L, ("i", t))
                    act.copy(v_rows[:, t, :], ps).then_inc(vrow_ready, 1)
                    att(L, ATT_AT[("i", t)])
                mods_behind(L, "i")
                for t in range(NT):
                    ps = sync_group(L, ("g", t))
                    act.activation(sg[:, t, :], ps, ACT.Sigmoid).then_inc(sig_done, 1)
                    if ("g", t) in ATT_AT:
                        att(L, ATT_AT[("g", t)])
                lev(L, 0)
                lev(L, 1)
                for j in range(KC):
                    ps = sync_group(L, ("ga", j))
                    act.activation(mergedT[:, j, :], ps[:, 0:TOK], ACT.Sigmoid).then_inc(ga_ready, 1)
                    lev(L, LEV_AT[("ga", j)] + 2)
                if L == 0:
                    for m in range(MOD_LEV, MOD_LATE, 2):
                        for i in range(2):
                            mod_copy(m + i)
                            if ("mod", m + i) in LEV_AT:
                                lev(L, LEV_AT[("mod", m + i)] + 2)
                        mod_store(m)
                        mod_store(m + 1)
                else:
                    for s in range(KC + 2, LEV_STEPS):
                        lev(L, s)
                act.wait_ge(lv_mm, LEV_TILES * L + NT * 14)
                act.activation(W[1].rearrange("p (s t) -> p s t", s=SEG), Cs[0][:, :, 1:129], ACT.Exp)
                for d in range(2):
                    ins = act.activation(dec[:, d, :], Cs[d][:, :, 128], ACT.Exp)
                ins.then_inc(fin_E, 1)
                act.wait_ge(fin_D, 2 * L + 1)
                act.activation(E[0], E[0], ACT.Exp).then_inc(fin_E, 1)
                act.wait_ge(fin_D, 2 * L + 2)
                act.activation(W[0], W[0], ACT.Exp).then_inc(fin_E, 1)
                act.wait_ge(lv_W, LEV_STEPS * (L + 1))
                act.activation(E[1].rearrange("p (s t) -> p s t", s=SEG), Cs[1][:, :, 0:128], ACT.Exp).then_inc(fin_E, 1)
                act.wait_ge(st_ready, 4 * L + 2)
                for d in range(2):
                    dst = (new_sf, new_sb)[d][0, L].rearrange("h k v -> k h v")
                    act.dma_start(dst, St_out[:, d, :, :]).then_inc(st_stored, 16)
                for t in range(NT):
                    act.wait_ge(o_mm, NT * L + t + 1)
                    act.activation(E[0][:, t * 512:(t + 1) * 512], bank[O_BANK[t]], ACT.Square).then_inc(o_sq, 1)
                for t in range(NT):
                    act.wait_ge(o_T, NT * L + t + 1)
                    act.copy(recT[:, :, t * P:(t + 1) * P],
                             bank[3 + t].rearrange("p (h t) -> p h t", h=HH)).then_inc(rec_ready, 1)
                for j in range(KC):
                    ps = sync_group(L, ("gh", j))
                    if j >= 2:
                        act.wait_ge(merged, KC * L + j - 1)
                    act.activation(gs[:, j % 2, :], ps[:, 0:TOK], ACT.Sigmoid).then_inc(gh_ready, 1)
                norm(L, 1)
                if L == 0:
                    mod_store(MOD_LATE)
                    mod_store(MOD_LATE + 1)
                    mod_copy(MOD_LATE + 2)
                act.wait_ge(rt_T, L + 1)
                act.activation(sc, bank[3][:, 0:NT * NE], ACT.Sigmoid).then_inc(rt_sc, 1)
                if L == 0:
                    mod_copy(MOD_LATE + 3)
                    mod_store(MOD_LATE + 2)
                    mod_store(MOD_LATE + 3)
                act.wait_ge(route_ready, L + 1)
                act.reg_mov(further_l, 0)
                with act.Fori(0, NE // 2) as p:
                    for j in range(2):
                        n = p * 2 + (L * NE + j)
                        act.wait_ge(e_gate, n + 1)
                        act.wait_ge(e_act, n + 1)
                        act.activation(gsil, bank[2][:, 0:256], ACT.Silu).then_inc(e_silu, 1)
                        act.wait_ge(e_down, n + 1)
                        act.wait_ge(e_ydma[j], (p + L * NE // 2) * 32 + Y0)
                        act.copy(ysb[j], bank[1]).then_inc(e_y, 1)
                        act.wait_ge(e_y, n + 2)
                        for hf in range(2):
                            act.dma_start(y_scr[bass.ds(p * (2 * BLK) + j * BLK, BLK), 512 * hf:512 * (hf + 1)],
                                          ysb[j][BLK * hf:BLK * (hf + 1), :]).then_inc(e_ydma[j], 16)
                        more = act.value_load(nov[0:1, bass.ds(p * 2 + j, 1)], min_val=0, max_val=5)
                        with act.If(more > 0):
                            with act.Fori(0, more):
                                b = act.snap(further)
                                act.wait_ge(v_pe, b * 5 + 6)
                                act.activation(gsil_o, bank[6][:, 0:256], ACT.Silu).then_inc(v_act, 1)
                                act.wait_ge(v_dve, b * 7 + 7)
                                row = act.snap(further_l, min_val=0, max_val=MAX_EXTRA - 1) * BLK + NE * BLK
                                for hf in range(2):
                                    act.dma_start(y_scr[bass.ds(row, BLK), 512 * hf:512 * (hf + 1)],
                                                  y_o[BLK * hf:BLK * (hf + 1), :]).then_inc(v_dma, 16)
                                act.reg_add(further, further, 1)
                                act.reg_add(further_l, further_l, 1)
                for j in range(2):
                    act.wait_ge(e_ydma[j], 32 * (NE // 2) * (L + 1) + Y0)
                act.wait_ge(v_dma, act.snap(further) * 32 + Y0)
                act.sem_inc(y_all, 1)

        @block.vector
        def _(dve):
            own = [0]

            def link(ins):
                own[0] += 1
                ins.then_inc(dve_own, 1)
                dve.wait_ge(dve_own, own[0])

            def sync_group(L, name):
                dve.wait_ge(group, gno(L, name) + 1)
                return bank[gno(L, name) % 2]

            def seg4(ap):
                return ap.rearrange("p (s t) -> p s t", s=SEG)

            dve.sem_inc(e_act, 1)
            dve.memset(half[:, :], -0.5)
            dve.memset(brow[:, :, :], 0.0)
            dve.memset(zeros, 0.0).then_inc(zeroed, 1)
            dve.wait_ge(prow_T, 1)
            for cnd in range(2):
                ins = dve.tensor_copy(cst[:, :, cnd, :], bc(bank[2][:, 8 * cnd:8 * cnd + 8], [P, KC, 16], 2))
            ins.then_inc(cst_ready, 1)
            link(dve.tensor_copy(lraw[:, :], bank[2][:, 16:32]))
            lr = lraw[:, :].rearrange("p (d l h) -> p l d h", d=2, l=DEPTH)
            lb4 = lbe[:, :, :].rearrange("p n (d h) -> p n d h", d=2)
            link(dve.tensor_tensor(lb4[:, 0], lr[:, 0], lr[:, 1], ALU.max))
            for l in range(DEPTH):
                ins = dve.tensor_tensor(lb4[:, 1 + l], lr[:, l], lb4[:, 0], ALU.subtract)
            ins.then_inc(lb_ready, 1)
            dve.wait_ge(lb_ready, 2)
            link(dve.tensor_tensor(lbe[:, 0, :], lbe[:, 1, :], lbe[:, 2, :], ALU.add))
            link(dve.reciprocal(lbe[:, 3, :], lbe[:, 0, :]))
            link(dve.tensor_tensor(lbe[:, 1, :], lbe[:, 1, :], lbe[:, 3, :], ALU.mult))
            link(dve.tensor_tensor(lbe[:, 2, :], lbe[:, 2, :], lbe[:, 3, :], ALU.mult))
            link(dve.tensor_tensor(lbe[:, 0, :], lbe[:, 1, :], lbe[:, 2, :], ALU.add))
            dve.tensor_tensor(lbT[:, 0].rearrange("p d h -> p (d h)"), lbe[:, 1, :], lbe[:, 1, :], ALU.subtract)
            link(dve.tensor_tensor(lbT[:, 1].rearrange("p d h -> p (d h)"), lbe[:, 0, :], lbe[:, 1, :], ALU.subtract))
            link(dve.tensor_scalar(omT[:, :, :, :].rearrange("p l d h -> p (l d h)"),
                                   lbT[:, :, :, :].rearrange("p l d h -> p (l d h)"), -1.0, 1.0, ALU.mult, ALU.add))

            def norm_scale(n):
                dve.wait_ge(mods_in, 16 * 4 * n)
                dve.wait_ge(nw_in, 16 * (n + 1))
                for cnd in range(2):
                    ins = dve.scalar_tensor_tensor(modb[:, 1, cnd, :], modb[:, 1, cnd, :], 1.0, nw[:, :],
                                                   ALU.add, ALU.mult)
                link(ins)

            def norm(L, which):
                n = 2 * L + which
                if which == 1:
                    norm_scale(n)
                dve.wait_ge(sq_done, NT * (n + 1))
                dve.tensor_scalar(stat[:, 0:NT], stat[:, 0:NT], 1.0 / D, EPS, ALU.mult, ALU.add).then_inc(ms_done, 1)
                dve.wait_ge(rstd_done, n + 1)
                for t in range(NT):
                    cnd = min(t, 1)
                    link(dve.scalar_tensor_tensor(hrow[:, t, :], xs[:, t, :], stat[:, t:t + 1], modb[:, 1, cnd, :],
                                                  ALU.mult, ALU.mult))
                    dve.tensor_tensor(hrow[:, t, :], hrow[:, t, :], modb[:, 0, cnd, :], ALU.add).then_inc(h_ready, 1)
                for t in range(NT):
                    dve.wait_ge(hT_made, 2 * NT * n + 2 * t + 1)
                    dve.tensor_copy(hT[:, 0:4, t * P:(t + 1) * P],
                                    bank[2 + 2 * t].rearrange("p (k t) -> p k t", k=4)).then_inc(hT_v, 1)

            def att(L, k):
                if k < ATT_STEPS:
                    nk = P if k % NT == 0 else 3 * P
                    c0 = 80 + 8 * (k % 2)
                    dve.wait_ge(at_scores, ATT_STEPS * L + k + 1)
                    link(dve.tensor_reduce(stat[:, c0:c0 + 2], pS[:, :, 0:nk], AX.X, ALU.max))
                    dve.tensor_scalar(stat[:, c0 + 2:c0 + 4], stat[:, c0:c0 + 2], -float(HD) ** -0.5, None,
                                      ALU.mult).then_inc(at_max, 1)
                    dve.wait_ge(at_exp, 2 * (ATT_STEPS * L + k + 1))
                    link(dve.reciprocal(stat[:, c0 + 6:c0 + 8], stat[:, c0 + 4:c0 + 6]))
                    for u in range(2):
                        x = prob[:, k % 2, u, 0:nk]
                        ins = dve.tensor_scalar(x, x, stat[:, c0 + 6 + u:c0 + 7 + u], None, ALU.mult)
                    ins.then_inc(at_prob, 1)
                if 1 <= k <= ATT_STEPS:
                    nk = P if (k - 1) % NT == 0 else 3 * P
                    dve.wait_ge(at_PT, ATT_STEPS * L + k)
                    if k >= 2:
                        dve.wait_ge(at_out, ATT_STEPS * L + k - 1)
                    dve.tensor_copy(PT[:, 0, 0:nk], bank[4][:, 0:nk]).then_inc(at_PTv, 1)
                if k >= 2:
                    r, t = (k - 2) // NT, (k - 2) % NT
                    dve.wait_ge(at_out, ATT_STEPS * L + k - 1)
                    dve.tensor_copy(attnT[:, r, t * P:(t + 1) * P], bank[6][:, 0:P]).then_inc(at_outv, 1)

            def lev(L, s):
                lev_mask(L, s - 2)
                if s < LEV_STEPS:
                    if s >= 2:
                        dve.wait_ge(lv_mm, LEV_TILES * L + NT * (s - 1))
                    if s < 2 * NLEV:
                        m, d = 64 >> (s // 2), s % 2
                        dve.wait_ge(lv_E, 2 * NLEV * L + s + 1)
                        Wv, Ev, qv, kv = (x.rearrange("p (s b u m) -> p s b u m", s=SEG, u=2, m=m)
                                          for x in (W[d], E[d], qh, kg[d]))
                        for u in range(2):
                            src = kv if u == d else qv
                            ins = dve.tensor_tensor(Wv[:, :, :, u, :], src[:, :, :, u, :], Ev[:, :, :, u, :], ALU.mult)
                    else:
                        ins = dve.tensor_tensor(W[0], kg[0], kg[1], ALU.add)
                    ins.then_inc(lv_W, 1)

            def lev_mask(L, s):
                if s >= 0:
                    for t in range(NT):
                        u = NT * s + t
                        dve.wait_ge(lv_mm, LEV_TILES * L + u + 1)
                        if u >= NT:
                            dve.wait_ge(lv_mask, LEV_TILES * L + u - 2)
                        A4 = AT.rearrange("p (h t) c -> p h t c", h=HH)[:, :, t, :]
                        dve.copy_predicated(A4, bc(masks[:, s, :], [P, HH, P], 1),
                                            bank[2 + u % 4].rearrange("p (h t) -> p h t", h=HH)).then_inc(lv_mask, 1)

            def wba(L, j):
                ps = sync_group(L, ("wba", j))
                dve.wait_ge(ga_ready, KC * (L + 1))
                dve.tensor_tensor(mergedT[:, j, :], ps[:, 0:TOK], mergedT[:, j, :], ALU.mult).then_inc(wba_done, 1)

            def fin(L, i, dst, src):
                dve.wait_ge(fin_E, 4 * L + i + 1)
                dve.tensor_tensor(dst, dst, src, ALU.mult).then_inc(fin_W, 1)

            def kd_evac(L, i):
                dve.wait_ge(kd_T, 4 * L + i + 1)
                dve.tensor_copy(kdT[i // 2][:, i % 2, :], bank[2 + i]).then_inc(kd_Tv, 1)

            dve.wait_ge(nw_in, 16)
            for m in range(MOD_FIRST):
                dve.wait_ge(mod_bc, m + 1)
                cut = slice(512 * (m % 2), 512 * (m % 2 + 1))
                for cnd in range(2):
                    ps, dst = bank[2 + 2 * (m % 3) + cnd], modb[:, m // 2, cnd, cut]
                    if m < 2:
                        ins = dve.tensor_copy(dst, ps)
                    else:
                        ins = dve.scalar_tensor_tensor(dst, ps, 1.0, nw[:, cut], ALU.add, ALU.mult)
                ins.then_inc(mod_bcv, 1)
            dve.wait_ge(mod_bcv, MOD_FIRST)
            further = dve.alloc_register("dve_further")
            dve.reg_mov(further, 0)

            for L in range(DEPTH):
                norm(L, 0)
                if L == 0:
                    dve.wait_ge(small_in, SMALL_LOADS)
                    dve.tensor_copy(masks[:, :, :].rearrange("p s t -> p (s t)"), masks32).then_inc(masks_ready, 1)
                    dve.wait_ge(masks_ready, 1)
                for d in range(2):
                    dve.memset(Cs[d][:, :, 0:1], 0.0)
                for n in range(2 * NT):
                    isq, t = n < NT, n % NT
                    heads = NQ if isq else NKV
                    ps = sync_group(L, ("q" if isq else "kv", t))
                    x = Q[:, t, :].rearrange("p (h d) -> p h d", h=NQ) if isq else Kd[:, t, :, 0, :]
                    ins = dve.tensor_copy(x, ps[:, 0:heads * HD].rearrange("p (h d) -> p h d", h=heads))
                    if not isq:
                        ins = dve.tensor_copy(Vt[:, t, :], ps[:, P:2 * P])
                    ins.then_inc(qkv_evac, 1)
                    dve.wait_ge(qkv_evac, 2 * NT * L + n + 1)
                    sq = scratch[:, 1024:1024 + heads * HD].rearrange("p (h d) -> p h d", h=heads)
                    link(dve.tensor_tensor(sq, x, x, ALU.mult))
                    ms = stat[:, 16 + 8 * n:16 + 8 * n + heads]
                    link(dve.tensor_reduce(ms, sq, AX.X, ALU.add))
                    dve.tensor_scalar(ms, ms, 1.0 / HD, EPS, ALU.mult, ALU.add).then_inc(qk_ms, 1)

                def hq(h):
                    ps = sync_group(L, ("hq", h))
                    dve.wait_ge(sig_done, (HH + NT) * L + h + 1)
                    x = qh[:, h * TOK:(h + 1) * TOK]
                    dve.scalar_tensor_tensor(x, ps[:, 0:TOK], float(HK) ** -0.5, x, ALU.mult,
                                             ALU.mult).then_inc(hgq_ready, 1)

                for h in range(HH - 1):
                    hq(h)
                for t in range(NT):
                    dve.wait_ge(qk_T, 5 * L + t + 1)
                    dve.tensor_copy(qTa[:, :, t * P:(t + 1) * P],
                                    bank[2 + t].rearrange("p (r t) -> p r t", r=4)).then_inc(qT_ready, 1)
                hq(HH - 1)
                att(L, 0)
                for d, kind in enumerate(("ff", "fb")):
                    for h in range(HH):
                        dve.wait_ge(f_sig, 2 * HH * L + HH * d + h + 1)
                        x = kg[d][:, h * TOK:(h + 1) * TOK]
                        dve.tensor_scalar(x, x, omT[:, L, d, h:h + 1], lbT[:, L, d, h:h + 1], ALU.mult,
                                          ALU.add).then_inc(f_done, 1)
                        att(L, ATT_AT[(kind, h)])
                    dve.wait_ge(ln_done, 2 * L + d + 1)
                    for s in range(SEG):
                        dve.tensor_tensor_scan(Cs[d][:, s, 1:129], ones, scratch[:, s * P:(s + 1) * P], 0.0,
                                               ALU.mult, ALU.add)
                    dve.tensor_scalar(kg[d], kg[d], -1.0, 1.0, ALU.mult, ALU.add).then_inc(C_ready, 1)
                for t in range(NT):
                    att(L, ATT_AT[("i", t)])
                for t in range(NT):
                    ps = sync_group(L, ("g", t))
                    dve.wait_ge(sig_done, (HH + NT) * L + HH + t + 1)
                    dve.tensor_tensor(sg[:, t, :], ps, sg[:, t, :], ALU.mult).then_inc(sg_mul, 1)
                    if ("g", t) in ATT_AT:
                        att(L, ATT_AT[("g", t)])
                dve.wait_ge(kv_stored, 16 * 2 * (L + 1))
                for s in range(LEV_STEPS + 2):
                    lev(L, s)
                fin(L, 0, W[1], qh)
                fin(L, 1, E[0], kg[0])
                wba(L, 0)
                fin(L, 2, W[0], qh)
                fin(L, 3, E[1], kg[1])
                kd_evac(L, 0)
                kd_evac(L, 1)
                wba(L, 1)
                kd_evac(L, 2)
                kd_evac(L, 3)
                wba(L, 2)
                for i, (d, b) in enumerate(((0, 2), (1, 4))):
                    dve.wait_ge(st_mm, 4 * L + i + 1)
                    dve.tensor_copy(St_out[:, d, :, :], bank[b].rearrange("p (h v) -> p h v", h=HH)).then_inc(st_ready, 1)
                dve.wait_ge(ctx_in, 16 * 5 * (L + 1))
                for d, b, t in ((0, 3, 1), (1, 5, 2)):
                    dve.wait_ge(st_mm, 4 * L + 3 + d)
                    for h in range(HH):
                        ins = dve.scalar_tensor_tensor(St2[:, d, h, :], St[:, d, h, :], dec[:, d, h * NT + t:h * NT + t + 1],
                                                       bank[b][:, h * P:(h + 1) * P], ALU.mult, ALU.add)
                    ins.then_inc(st_ready, 1)
                wba(L, 3)
                for t in range(NT):
                    dve.wait_ge(o_sq, NT * L + t + 1)
                    ms = stat[:, 64 + 4 * t:68 + 4 * t]
                    link(dve.tensor_reduce(ms, E[0][:, t * 512:(t + 1) * 512].rearrange("p (h v) -> p h v", h=HH),
                                           AX.X, ALU.add))
                    dve.tensor_scalar(ms, ms, 1.0 / HK, EPS, ALU.mult, ALU.add).then_inc(o_ms, 1)
                wba(L, 4)
                wba(L, 5)
                for t in range(NT):
                    dve.wait_ge(o_rstd, NT * L + t + 1)
                    dve.wait_ge(sg_ready, NT * L + t + 1)
                    o4 = orow[:, t, :].rearrange("p (h v) -> p h v", h=HH)
                    link(dve.tensor_tensor(o4, bank[O_BANK[t]].rearrange("p (h v) -> p h v", h=HH),
                                           bc(stat[:, 64 + 4 * t:68 + 4 * t], [P, HH, HK], 2), ALU.mult))
                    dve.tensor_tensor(orow[:, t, :], orow[:, t, :], sg[:, t, :], ALU.mult).then_inc(o_ready, 1)
                wba(L, 6)
                wba(L, 7)
                for j in range(KC):
                    ps = sync_group(L, ("wbh", j))
                    dve.wait_ge(gh_ready, KC * L + j + 1)
                    dve.tensor_tensor(gs[:, j % 2, :], ps[:, 0:TOK], gs[:, j % 2, :], ALU.mult).then_inc(wbh_done, 1)
                    dve.wait_ge(wbh_done, KC * L + j + 1)
                    dve.tensor_tensor(mergedT[:, j, :], mergedT[:, j, :], gs[:, j % 2, :], ALU.add).then_inc(merged, 1)
                dve.wait_ge(gate_in, 16 * (4 * L + 2))
                for n in range(2 * NT):
                    i, t = n // NT, n % NT
                    ps = sync_group(L, ("wo", n))
                    dve.tensor_tensor(wo_tmp[:, n % 2, :], ps, modb[:, 2, min(t, 1), 512 * i:512 * (i + 1)],
                                      ALU.mult).then_inc(wo_evac, 1)
                    dve.wait_ge(wo_evac, 2 * NT * L + n + 1)
                    x = xs[:, t, 512 * i:512 * (i + 1)]
                    dve.tensor_tensor(x, x, wo_tmp[:, n % 2, :], ALU.add).then_inc(x_mid, 1)
                norm(L, 1)
                def one_hot(dst, where, done):
                    for t in range(NT):
                        ins = dve.tensor_scalar(dst[:, t, :], iota, where[:, t:t + 1] if len(where.shape) == 2
                                                else where[:, t, :], None, ALU.is_equal)
                    ins.then_inc(done, 1)

                def xT_view(dst):
                    return dst.rearrange("p (a c) s -> p c a s", a=2)

                def xT_src(b):
                    return bank[b].rearrange("p (c a s) -> p c a s", c=4, a=2)

                def aT_dst(dst):
                    return dst.rearrange("p (a c) s -> p c a s", a=2)

                def aT_src(b):
                    return bank[b][:, 0:256].rearrange("p (c a s) -> p c a s", c=2, a=2)

                dve.wait_ge(st_stored, 16 * 2 * (L + 1))
                dve.wait_ge(rt_log, L + 1)
                dve.tensor_copy(rlog[0:NE, :], bank[2][0:NE, 0:TOK]).then_inc(rt_logv, 1)
                dve.wait_ge(rt_sc, L + 1)

                def t3(x):
                    return x.rearrange("p (t e) -> p t e", t=NT)

                def ranks(out, x, n):
                    xv = x.rearrange("p (n i) -> p n i", i=4)
                    xi = xv.unsqueeze(2).broadcast_to([P, n, 4, 4])
                    xj = xv.unsqueeze(3).broadcast_to([P, n, 4, 4])
                    a4 = cmp1[:, 0:16 * n].rearrange("p (n j i) -> p n j i", j=4, i=4)
                    b4 = cmp2[:, 0:16 * n].rearrange("p (n j i) -> p n j i", j=4, i=4)
                    before = const[:, C_BEFORE:C_BEFORE + 16]
                    dve.tensor_tensor(a4, xi, xj, ALU.is_gt)
                    link(dve.tensor_tensor(b4, xi, xj, ALU.is_equal))
                    b3 = cmp2[:, 0:16 * n].rearrange("p (n c) -> p n c", c=16)
                    link(dve.tensor_tensor(b3, b3, bc(before, [P, n, 16], 1), ALU.mult))
                    link(dve.tensor_tensor(cmp1[:, 0:16 * n], cmp1[:, 0:16 * n], cmp2[:, 0:16 * n], ALU.add))
                    link(dve.tensor_reduce(out.rearrange("p (n j) -> p n j", j=4), a4, AX.X, ALU.add))

                link(dve.tensor_tensor(t3(sel), t3(sc), bc(br[:, :], [P, NT, NE], 1), ALU.add))
                ranks(rank, sel, NT * NG)
                link(dve.scalar_tensor_tensor(top, rank, 1.5, sel, ALU.is_lt, ALU.mult))
                link(dve.tensor_reduce(gsum, top.rearrange("p (n j) -> p n j", j=4), AX.X, ALU.add))
                ranks(grank, gsum, NT)
                link(dve.tensor_scalar(gb, grank, 0.5, None, ALU.is_lt))
                gbb = bc(gb, [P, NT * NG, 4], 2)
                for val, oh in ((0.0, oh0), (1.0, oh1)):
                    ins = dve.scalar_tensor_tensor(oh.rearrange("p (n j) -> p n j", j=4),
                                                   rank.rearrange("p (n j) -> p n j", j=4), val, gbb,
                                                   ALU.is_equal, ALU.mult)
                link(ins)
                dve.tensor_tensor(selm, oh0, oh1, ALU.add).then_inc(rt_sel, 1)
                dve.wait_ge(rt_sel, L + 1)
                link(dve.tensor_tensor(t48, sc, selm, ALU.mult))
                link(dve.tensor_reduce(wsum, t3(t48), AX.X, ALU.add))
                link(dve.reciprocal(wrec, wsum))
                for c, oh in enumerate((oh0, oh1)):
                    link(dve.tensor_tensor(t48, sc, oh, ALU.mult))
                    link(dve.tensor_reduce(wgt[:, c, :], t3(t48), AX.X, ALU.add))
                    link(dve.tensor_tensor(wgt[:, c, :], wgt[:, c, :], wrec, ALU.mult))
                dve.wait_ge(rt_pos, L + 1)
                dve.tensor_copy(pos, bank[4][:, 0:NT * NE])
                link(dve.tensor_copy(cnt, bank[4][:, NT * NE:NT * NE + NE]))
                dve.memset(posm, FAR)
                link(dve.tensor_scalar(t48, selm, -FAR, FAR, ALU.mult, ALU.add))
                link(dve.tensor_tensor(posm[:, :, 0:NE], t3(pos), t3(t48), ALU.add))
                one_hot(Pm, posm[:, :, 0:1], e_P)
                link(dve.tensor_scalar(novf, cnt, float(BLK), None, ALU.is_gt))
                for b in range(2, TOK // BLK):
                    link(dve.scalar_tensor_tensor(novf, cnt, float(BLK * b), novf, ALU.is_gt, ALU.add))
                dve.tensor_copy(nov[:, :], novf[0:1, :])
                link(dve.tensor_tensor_scan(ovs, ones[:, 0:NE], novf, 0.0, ALU.mult, ALU.add))
                link(dve.tensor_tensor(ovs, ovs, novf, ALU.subtract))
                link(dve.scalar_tensor_tensor(ob, ovs, float(BLK), const[:, C_OB:C_OB + NE], ALU.mult, ALU.add))
                link(dve.scalar_tensor_tensor(t3(idxa), t3(pos), float(BLK), bc(ob, [P, NT, NE], 1),
                                              ALU.is_ge, ALU.mult))
                link(dve.tensor_tensor(idxa, idxa, pos, ALU.add))
                link(dve.tensor_tensor(t3(idxa), t3(idxa), bc(const[:, C_E64:C_E64 + NE], [P, NT, NE], 1), ALU.add))
                for c, oh in enumerate((oh0, oh1)):
                    link(dve.tensor_tensor(t48, idxa, oh, ALU.mult))
                    link(dve.tensor_reduce(idxf[:, NT * c:NT * (c + 1)], t3(t48), AX.X, ALU.add))
                dve.tensor_copy(idx[:, :, :].rearrange("p c t -> p (c t)"), idxf).then_inc(route_ready, 1)
                dve.wait_ge(route_ready, L + 1)

                dve.wait_ge(e_gather, NGATH * L + 1)
                dve.tensor_copy(xrow, bank[0]).then_inc(e_xrow, 1)
                one_hot(Pm, posm[:, :, 1:2], e_P)
                dve.wait_ge(e_xTp, NGATH * L + 1)
                dve.tensor_copy(xT_view(xT[0]), xT_src(4)).then_inc(e_xT, 1)
                with dve.Fori(0, NE // 2) as p:
                    for j in range(2):
                        n = p * 2 + (L * NE + j)
                        m = p * 2 + (L * NGATH + j)
                        dve.wait_ge(e_up, n + 1)
                        dve.wait_ge(e_silu, n + 2)
                        dve.tensor_tensor(actb, bank[3][:, 0:256], gsil, ALU.mult).then_inc(e_act, 1)
                        dve.wait_ge(e_gather, m + 2)
                        dve.tensor_copy(xrow, bank[0]).then_inc(e_xrow, 1)
                        one_hot(Pm, posm[:, :, bass.ds(p * 2 + (j + 2), 1)], e_P)
                        dve.wait_ge(e_aTp, n + 1)
                        dve.tensor_copy(aT_dst(aT), aT_src(5)).then_inc(e_aT, 1)
                        dve.wait_ge(e_xTp, m + 2)
                        dve.tensor_copy(xT_view(xT[1 - j]), xT_src(4)).then_inc(e_xT, 1)
                        dve.tensor_scalar(pv.unsqueeze(2), posm[:, :, bass.ds(p * 2 + j, 1)], 1.0, None,
                                          ALU.mult).then_inc(e_own, 1)
                        dve.wait_ge(e_own, n + 1)
                        more = dve.value_load(nov[0:1, bass.ds(p * 2 + j, 1)], min_val=0, max_val=5)
                        with dve.If(more > 0):
                            with dve.Fori(0, more):
                                b = dve.snap(further)
                                dve.tensor_scalar(pv, pv, -float(BLK), None, ALU.add).then_inc(v_dve, 1)
                                dve.wait_ge(v_dve, b * 7 + 1)
                                one_hot(Pov, pv, v_dve)
                                dve.wait_ge(v_pe, b * 5 + 4)
                                dve.tensor_copy(xrow_o, bank[6]).then_inc(v_dve, 1)
                                dve.wait_ge(v_pe, b * 5 + 5)
                                dve.tensor_copy(xT_view(xT_o), xT_src(7)).then_inc(v_dve, 1)
                                dve.wait_ge(v_pe, b * 5 + 6)
                                dve.wait_ge(v_act, b + 1)
                                dve.tensor_tensor(act_o, bank[7][:, 0:256], gsil_o, ALU.mult).then_inc(v_dve, 1)
                                dve.wait_ge(v_pe, b * 5 + 7)
                                dve.tensor_copy(aT_dst(aT_o), aT_src(6)).then_inc(v_dve, 1)
                                dve.wait_ge(v_pe, b * 5 + 8)
                                dve.wait_ge(v_dma, b * 32 + Y0)
                                dve.tensor_copy(y_o, bank[7]).then_inc(v_dve, 1)
                                dve.reg_add(further, further, 1)
                if L + 1 < DEPTH:
                    norm_scale(2 * (L + 1))
                dve.wait_ge(gate_in, 16 * (4 * L + 4))
                for t in range(NT):
                    dve.wait_ge(yg_in[t], 32 * (L + 1))
                    y0, y1 = results[:, t, 0, :], results[:, t, 1, :]
                    link(dve.tensor_scalar(y0, y0, wgt[:, 0, t:t + 1], None, ALU.mult))
                    link(dve.scalar_tensor_tensor(y0, y1, wgt[:, 1, t:t + 1], y0, ALU.mult, ALU.add))
                    link(dve.tensor_tensor(y0, y0, modb[:, 2, min(t, 1), :], ALU.mult))
                    dve.tensor_tensor(xs[:, t, :], xs[:, t, :], y0, ALU.add).then_inc(x_done, 1)

        @block.tensor
        def _(pe):
            def transpose(out, in_, n=P):
                return pe.transpose(out, in_, ident[0:n, 0:n])

            def unit_in(L, name):
                s, n = landed_n(L, name)
                pe.wait_ge(landed[s], n)
                if name[0] in ("wba", "wbh"):
                    return ring[:, s, :].rearrange("p (k n) -> p k n", k=4)
                return ring[:, s, :].rearrange("p (k n) -> p k n", k=KC)

            def bank_read(n):
                L, (kind, i) = ALL_GROUPS[n]
                s, count = EVAC[kind](L, i)
                pe.wait_ge(s, count)

            def start_group(L, name):
                n = gno(L, name)
                if n >= 2:
                    bank_read(n - 2)
                return bank[n % 2]

            def finish_group(ins):
                ins.then_inc(group, 1)

            def mod(m):
                w = unit_in(0, ("mod", m))
                ps = start_group(0, ("mod", m))
                if m == 0:
                    pe.wait_ge(layer_in, 16 * DEPTH)
                for k in range(KC // 4):
                    for q in range(4):
                        pe.matmul(ps[32 * q:32 * q + 32, :], cst[:, 2 * q + k, :, :].rearrange("p c r -> p (c r)"),
                                  w[:, 2 * q + k, :], start=(k == 0), stop=(k == 1 and q > 0))
                for j in range(4):
                    r = 4 * (m % MODS) + j
                    ins = pe.matmul(ps[0:32, P * j:P * (j + 1)], ident[:, r:r + 1].broadcast_to([P, 32]),
                                    brow[:, m // MODS, :], start=False, stop=(j == 3))
                finish_group(ins)

            def mod_sum(m):
                ps = start_group(0, ("ms", m))
                pe.wait_ge(mod_evac, m + 1)
                finish_group(pe.matmul(ps[0:32, :], const[:, C_SEL:C_SEL + 32], mod_parts(m),
                                       start=True, stop=True))

            def mods_behind(L, kind):
                if L == 0 and kind in MOD_BEHIND:
                    m = MOD_BEHIND[kind]
                    mod(m)
                    mod(m + 1)
                    mod_sum(m)
                    mod_sum(m + 1)

            def mod_broadcast(m):
                pe.wait_ge(mod_evac, m + 1)
                if m >= 3:
                    pe.wait_ge(mod_bcv, m - 2)
                for cnd in range(2):
                    c0 = C_SEL + 16 * cnd
                    ins = pe.matmul(bank[2 + 2 * (m % 3) + cnd], const[:, c0:c0 + 1].broadcast_to([P, P]),
                                    mod_parts(m), start=True, stop=True)
                ins.then_inc(mod_bc, 1)

            def rows(L, name, w, width, t):
                ps = start_group(L, name)
                for k in range(KC):
                    ins = pe.matmul(ps[:, 0:width], hT[:, k, t * P:(t + 1) * P], w[:, k, 0:width],
                                    start=(k == 0), stop=(k == KC - 1))
                finish_group(ins)

            def cols(L, name, w, c0, src, nk):
                ps = start_group(L, name)
                for k in range(nk):
                    ins = pe.matmul(ps[:, 0:TOK], w[:, k, c0:c0 + P], src[:, k, :], start=(k == 0), stop=(k == nk - 1))
                finish_group(ins)

            def norm(L, which):
                n = 2 * L + which
                for t in range(NT):
                    pe.wait_ge(h_ready, NT * n + t + 1)
                    for hf in range(2):
                        for c in range(4):
                            k = 4 * hf + c
                            ins = transpose(bank[2 + 2 * t + hf][:, P * c:P * (c + 1)], hrow[:, t, P * k:P * (k + 1)])
                        ins.then_inc(hT_made, 1)
                pe.wait_ge(hT_v, NT * (n + 1))
                pe.wait_ge(hT_a, NT * (n + 1))

            def att(L, k):
                if k < ATT_STEPS:
                    r, t = k // NT, k % NT
                    k0, nk = (0, P) if t == 0 else (P, 3 * P)
                    if k >= 1:
                        pe.wait_ge(at_exp, 2 * (ATT_STEPS * L + k))
                    for u in range(2):
                        ins = pe.matmul(bank[2 + u][:, 0:nk], qTa[64 * u:64 * u + 64, r, t * P:(t + 1) * P],
                                        kT[64 * u:64 * u + 64, r // 2, k0:k0 + nk], start=True, stop=True)
                    ins.then_inc(at_scores, 1)
                if 1 <= k <= ATT_STEPS:
                    nb = 1 if (k - 1) % NT == 0 else 3
                    pe.wait_ge(at_prob, ATT_STEPS * L + k)
                    if k >= 2:
                        pe.wait_ge(at_PTv, ATT_STEPS * L + k - 1)
                        pe.wait_ge(at_PTa, ATT_STEPS * L + k - 1)
                    for u in range(2):
                        for b in range(nb):
                            ins = transpose(bank[4 + u][:, P * b:P * (b + 1)], prob[:, (k - 1) % 2, u, P * b:P * (b + 1)])
                    ins.then_inc(at_PT, 1)
                if k >= 2:
                    kk = k - 2
                    r, t = kk // NT, kk % NT
                    blocks = [0] if t == 0 else [1, 2, 3]
                    pe.wait_ge(at_PTv, ATT_STEPS * L + kk + 1)
                    pe.wait_ge(at_PTa, ATT_STEPS * L + kk + 1)
                    if kk >= 1:
                        pe.wait_ge(at_outv, ATT_STEPS * L + kk)
                    g0 = HD * (r // 2)
                    for u in range(2):
                        for i, b in enumerate(blocks):
                            ins = pe.matmul(bank[6][64 * u:64 * u + 64, 0:P], Vt[:, b, g0:g0 + HD],
                                            PT[:, u, P * i:P * (i + 1)], start=(i == 0), stop=(i == len(blocks) - 1))
                    ins.then_inc(at_out, 1)

            def lev(L, s):
                pe.wait_ge(lv_W, LEV_STEPS * L + s + 1)
                for t in range(NT):
                    u = NT * s + t
                    if u >= 4:
                        pe.wait_ge(lv_mask, LEV_TILES * L + u - 3)
                    for h in range(HH):
                        c = (h * NT + t) * P
                        lhs = W[s % 2][:, c:c + P]
                        rhs = lhs if s < 2 * NLEV else qh[:, c:c + P]
                        ins = pe.matmul(bank[2 + u % 4][:, P * h:P * (h + 1)], lhs, rhs, start=True, stop=True)
                    ins.then_inc(lv_mm, 1)

            def kd(L, i):
                d, t = i // 2, ((0, 1), (0, 2))[i // 2][i % 2]
                pe.wait_ge(fin_W, 4 * L + (2 if d == 0 else 4))
                pe.wait_ge(lv_mask, LEV_TILES * (L + 1))
                for h in range(HH):
                    c = (h * NT + t) * P
                    ins = transpose(bank[2 + i][:, P * h:P * (h + 1)], E[d][:, c:c + P])
                ins.then_inc(kd_T, 1)

            def block64(dst_gate, dst_up, x, wg, wu):
                last = []
                for dst, w in ((dst_gate, wg), (dst_up, wu)):
                    if w is None:
                        continue
                    for k in range(KC):
                        for hf in range(2):
                            ins = pe.matmul(dst[64 * hf:64 * hf + 64, 0:256], x[:, k, :], w[:, k, 256 * hf:256 * (hf + 1)],
                                            start=(k == 0), stop=(k == KC - 1))
                    last.append(ins)
                return last[-1]

            def gather64(dst, sel1):
                for t in range(NT):
                    for hf in range(2):
                        ins = pe.matmul(dst[64 * hf:64 * hf + 64, :], sel1[:, t, :], hrow[:, t, 512 * hf:512 * (hf + 1)],
                                        start=(t == 0), stop=(t == NT - 1))
                return ins

            def down64(dst, x, w):
                for k in range(4):
                    for hf in range(2):
                        ins = pe.matmul(dst[64 * hf:64 * hf + 64, :], x[:, k, :], w[:, k, 512 * hf:512 * (hf + 1)],
                                        start=(k == 0), stop=(k == 3))
                return ins

            def turn(dst, src, n):
                for c in range(n):
                    ins = transpose(dst[:, P * c:P * (c + 1)], src[:, P * c:P * (c + 1)])
                return ins

            further = pe.alloc_register("pe_further")
            pe.reg_mov(further, 0)
            pe.sem_inc(v_pe, V0)
            pe.wait_ge(setup_in, 16 * 5)
            pe.wait_ge(prow_silu, 1)
            transpose(bank[2][:, 0:32], prow[:, :], 32).then_inc(prow_T, 1)
            pe.wait_ge(cst_ready, 1)

            for L in range(DEPTH):
                if L > 0:
                    pe.wait_ge(e_xrow, NGATH * L)
                    pe.wait_ge(e_y, NE * L + 1)
                else:
                    for m in range(MOD_FIRST):
                        mod(m)
                        if m > 0:
                            mod_broadcast(m - 1)
                    mod_broadcast(MOD_FIRST - 1)
                norm(L, 0)
                w = unit_in(L, ("q", 0))
                for t in range(NT):
                    rows(L, ("q", t), w, 512, t)
                w = unit_in(L, ("kv", 0))
                for t in range(NT):
                    rows(L, ("kv", t), w, 256, t)
                w = unit_in(L, ("hq", 0))
                for h in range(HH - 1):
                    cols(L, ("hq", h), w, P * h, hT, KC)
                for t in range(NT):
                    pe.wait_ge(qk_ready, 2 * NT * L + t + 1)
                    turn(bank[2 + t], Q[:, t, :], 4).then_inc(qk_T, 1)
                pe.wait_ge(qk_ready, 2 * NT * (L + 1))
                pe.wait_ge(ctx_in, 16 * 5 * (L + 1))
                for gk in range(NKV):
                    for b in range(4):
                        ins = transpose(bank[5 + gk][:, P * b:P * (b + 1)],
                                        Kd[:, b, gk, :, :].rearrange("p u d -> p (u d)"))
                    ins.then_inc(qk_T, 1)
                cols(L, ("hq", HH - 1), w, P * (HH - 1), hT, KC)
                pe.wait_ge(qT_ready, NT * (L + 1))
                pe.wait_ge(kT_ready, NKV * (L + 1))
                att(L, 0)
                mods_behind(L, "hq")
                for kind in ("ff", "fb"):
                    w = unit_in(L, (kind, 0))
                    for h in range(HH):
                        cols(L, (kind, h), w, P * h, hT, KC)
                        att(L, ATT_AT[(kind, h)])
                    mods_behind(L, kind)
                for kind in ("i", "g"):
                    w = unit_in(L, (kind, 0))
                    for t in range(NT):
                        rows(L, (kind, t), w, 512, t)
                        if (kind, t) in ATT_AT:
                            att(L, ATT_AT[(kind, t)])
                    mods_behind(L, kind)
                pe.wait_ge(at_outv, ATT_STEPS * (L + 1))
                for j in range(KC):
                    if j % 4 == 0:
                        w = unit_in(L, ("ga", j // 4))
                    cols(L, ("ga", j), w, P * (j % 4), hT, KC)
                    lev(L, LEV_AT[("ga", j)])
                if L == 0:
                    for m in range(MOD_LEV, MOD_LATE, 2):
                        for i in range(2):
                            mod(m + i)
                            if ("mod", m + i) in LEV_AT:
                                lev(L, LEV_AT[("mod", m + i)])
                        mod_sum(m)
                        mod_sum(m + 1)
                else:
                    for s in range(KC, LEV_STEPS):
                        lev(L, s)
                w = unit_in(L, ("wba", 0))
                for j in range(KC):
                    cols(L, ("wba", j), w, P * j, attnT, 4)
                    if j == 0:
                        kd(L, 0)
                        kd(L, 1)
                    if j == 1:
                        kd(L, 2)
                        kd(L, 3)
                    if j == 2:
                        pe.wait_ge(vrow_ready, NT * (L + 1))
                        for d, b, i, t in ((0, 2, 0, 0), (1, 4, 2, 0), (0, 3, 1, 1), (1, 5, 3, 2)):
                            pe.wait_ge(kd_Tv, 4 * (L + 1))
                            for h in range(HH):
                                ins = pe.matmul(bank[b][:, P * h:P * (h + 1)], kdT[d][:, i % 2, P * h:P * (h + 1)],
                                                v_rows[:, t, P * h:P * (h + 1)], start=True, stop=True)
                            ins.then_inc(st_mm, 1)
                    if j == 3:
                        for t in range(NT):
                            if t > 0:
                                pe.wait_ge(st_ready, 4 * (L + 1))
                            for h in range(HH):
                                sgm = h * NT + t
                                out = bank[O_BANK[t]][:, P * h:P * (h + 1)]
                                ins = pe.matmul(out, AT[:, sgm, :], v_rows[:, t, P * h:P * (h + 1)], start=True,
                                                stop=(t == 0))
                                if t > 0:
                                    s_f, s_b = (St, St2) if t == 1 else (St2, St)
                                    pe.matmul(out, W[1][:, sgm * P:(sgm + 1) * P], s_f[:, 0, h, :], start=False, stop=False)
                                    ins = pe.matmul(out, W[0][:, sgm * P:(sgm + 1) * P], s_b[:, 1, h, :], start=False,
                                                    stop=True)
                            ins.then_inc(o_mm, 1)
                for t in range(NT):
                    pe.wait_ge(o_ready, NT * L + t + 1)
                    turn(bank[3 + t], orow[:, t, :], 4).then_inc(o_T, 1)
                pe.wait_ge(rec_ready, NT * (L + 1))
                wh = unit_in(L, ("gh", 0))
                wb = None
                for j in range(KC):
                    if j == 4:
                        wh = unit_in(L, ("gh", 1))
                    cols(L, ("gh", j), wh, P * (j % 4), hT, KC)
                    if wb is None:
                        wb = unit_in(L, ("wbh", 0))
                    cols(L, ("wbh", j), wb, P * j, recT, HH)
                pe.wait_ge(merged, KC * (L + 1))
                for n in range(2 * NT):
                    i, t = n // NT, n % NT
                    if t == 0:
                        w = unit_in(L, ("wo", i))
                    ps = start_group(L, ("wo", n))
                    for k in range(KC):
                        ins = pe.matmul(ps, mergedT[:, k, t * P:(t + 1) * P], w[:, k, :], start=(k == 0), stop=(k == KC - 1))
                    finish_group(ins)
                if L == 0:
                    mod(MOD_LATE)
                    mod(MOD_LATE + 1)
                norm(L, 1)
                for k in range(KC):
                    ins = pe.matmul(bank[2][0:NE, 0:TOK], wr[:, k, :], hT[:, k, :], start=(k == 0), stop=(k == KC - 1))
                ins.then_inc(rt_log, 1)
                if L == 0:
                    mod_sum(MOD_LATE)
                    mod_sum(MOD_LATE + 1)
                    mod(MOD_LATE + 2)
                pe.wait_ge(rt_logv, L + 1)
                for t in range(NT):
                    ins = transpose(bank[3][:, NE * t:NE * (t + 1)], rlog[0:NE, P * t:P * (t + 1)], NE)
                ins.then_inc(rt_T, 1)
                if L == 0:
                    mod(MOD_LATE + 3)
                pe.wait_ge(rt_sel, L + 1)
                for t in range(NT + 1):
                    before = list(range(min(t, NT)))
                    for i, tt in enumerate(before):
                        ins = pe.matmul(bank[4][:, NE * t:NE * (t + 1)], ones, selm[:, NE * tt:NE * (tt + 1)],
                                        start=(i == 0), stop=(t == NT and i == NT - 1))
                    if t < NT:
                        ins = pe.matmul(bank[4][:, NE * t:NE * (t + 1)], tri, selm[:, NE * t:NE * (t + 1)],
                                        start=(t == 0), stop=True)
                ins.then_inc(rt_pos, 1)
                if L == 0:
                    mod_sum(MOD_LATE + 2)
                    mod_sum(MOD_LATE + 3)
                pe.wait_ge(e_P, NPOS * L + 1)
                for i in range(2):
                    bank_read(gno(L, GROUPS[L][-1]) - i)
                gather64(bank[0], Pm).then_inc(e_gather, 1)
                pe.wait_ge(e_xrow, NGATH * L + 1)
                turn(bank[4], xrow, 4).then_inc(e_xTp, 1)
                pe.wait_ge(route_ready, L + 1)
                with pe.Fori(0, NE // 2) as p:
                    for j in range(2):
                        n = p * 2 + (L * NE + j)
                        m = p * 2 + (L * NGATH + j)
                        wg, wu = (ring[:, 3 * j + i, :].rearrange("p (k n) -> p k n", k=KC) for i in range(2))
                        wd = ring[:, 3 * j + 2, :].rearrange("p (k n) -> p k n", k=4)
                        pe.wait_ge(e_xT, m + 1)
                        pe.wait_ge(landed[3 * j], landed_e(L, 3 * j, p))
                        pe.wait_ge(e_silu, n + 1)
                        block64(bank[2], None, xT[j], wg, None).then_inc(e_gate, 1)
                        pe.wait_ge(landed[3 * j + 1], landed_e(L, 3 * j + 1, p))
                        pe.wait_ge(e_act, n + 1)
                        block64(None, bank[3], xT[j], None, wu).then_inc(e_up, 1)
                        pe.wait_ge(e_P, p * 2 + (L * NPOS + j + 2))
                        pe.wait_ge(e_xrow, m + 1)
                        gather64(bank[0], Pm).then_inc(e_gather, 1)
                        pe.wait_ge(e_act, n + 2)
                        turn(bank[5], actb, 2).then_inc(e_aTp, 1)
                        pe.wait_ge(e_xrow, m + 2)
                        turn(bank[4], xrow, 4).then_inc(e_xTp, 1)
                        pe.wait_ge(e_aT, n + 1)
                        pe.wait_ge(landed[3 * j + 2], landed_e(L, 3 * j + 2, p))
                        pe.wait_ge(e_y, n + 1)
                        down64(bank[1], aT, wd).then_inc(e_down, 1)
                        more = pe.value_load(nov[0:1, bass.ds(p * 2 + j, 1)], min_val=0, max_val=5)
                        with pe.If(more > 0):
                            with pe.Fori(0, more):
                                b = pe.snap(further)
                                pe.wait_ge(v_dve, b * 7 + 2)
                                gather64(bank[6], Pov).then_inc(v_pe, 1)
                                pe.wait_ge(v_dve, b * 7 + 3)
                                turn(bank[7], xrow_o, 4).then_inc(v_pe, 1)
                                pe.wait_ge(v_dve, b * 7 + 4)
                                block64(bank[6], bank[7], xT_o, wg, wu).then_inc(v_pe, 1)
                                pe.wait_ge(v_dve, b * 7 + 5)
                                turn(bank[6], act_o, 2).then_inc(v_pe, 1)
                                pe.wait_ge(v_dve, b * 7 + 6)
                                down64(bank[7], aT_o, wd).then_inc(v_pe, 1)
                                pe.reg_add(further, further, 1)


_INS = ["x_prompt", "x_sample", "cache_k", "cache_v", "state_fwd", "state_bwd", "c", "c_ctx", "norm1_w", "norm2_w",
        "w_mod", "b_mod", "w_in", "q_norm_w", "k_norm_w", "hgrn_lb_fwd", "hgrn_lb_bwd", "hgrn_norm_w", "w_br_attn",
        "w_br_hgrn", "w_out", "w_router", "b_router", "w_exp_gate", "w_exp_up", "w_exp_down"]
_OUTS = [(1, P, D), (1, 2 * P, D), (1, DEPTH, NKV, P, HD), (1, DEPTH, NKV, P, HD),
         (1, DEPTH, HH, HK, HK), (1, DEPTH, HH, HK, HK)]


def kernel(**inputs):
    import numpy as _np
    import concourse.bacc as _bacc
    from concourse import mybir as _mybir
    from concourse.bass_utils import run_bass_kernel_spmd as _run

    nc = _bacc.Bacc("TRN2", target_bir_lowering=False, num_devices=1)
    arrays, aps = {}, {}

    def given(name, a):
        arrays[f"in_{name}_dram"] = a
        aps[name] = nc.dram_tensor(f"in_{name}_dram", a.shape, _mybir.dt.from_np(a.dtype), kind="ExternalInput").ap()

    for name in _INS:
        given(name, _np.ascontiguousarray(inputs[name]))
    consts, masks = shape_constants()
    given("consts", consts)
    given("masks", masks)
    outs = [nc.dram_tensor(f"out_{i}_dram", s, F32, kind="ExternalOutput").ap() for i, s in enumerate(_OUTS)]
    build(nc, aps, outs)
    r = _run(nc, [arrays], core_ids=[0])
    return tuple(r.results[0][f"out_{i}_dram"] for i in range(len(_OUTS)))
```
